# Optimizing a Trainium2 kernel written in Bass

```python
import jax, jax.numpy as jnp
from jax import lax
import numpy as np

D_MODEL = 1024
BATCH = 1
SEQ = 512
DEPTH = 2
DEC_BATCH = 8
DEC_SEQ = 8
PAST_LEN = 2048
PAGE_SIZE = 128

N_EVEN = (DEPTH + 1) // 2
N_ODD = DEPTH // 2
ALPHA = (2 * DEPTH) ** 0.25
BETA = (8 * DEPTH) ** -0.25
LN_EPS = 1e-5
RMS_EPS = 1e-6
F32 = jnp.float32

A_WIDTH = D_MODEL // 2
POOL_WINDOWS = (2, 4, 8, 16)
A_GROUPS = len(POOL_WINDOWS)
A_GROUP_DIM = A_WIDTH // A_GROUPS
POOL_BUF = max(POOL_WINDOWS) - 1
B_WIDTH = D_MODEL // 2
B_HEADS = 4
B_HEAD_DIM = B_WIDTH // B_HEADS
CHUNK = 128
EVEN_IN = A_WIDTH + 2 * B_WIDTH
C_WIDTH = D_MODEL // 2
C_HEAD_DIM = 64
C_HEADS = C_WIDTH // C_HEAD_DIM
C_DECAY_LORA = 64
C_ICLR_LORA = 64
C_GATE_LORA = 128
C_COLS = 3 * C_WIDTH + C_DECAY_LORA + C_ICLR_LORA + C_GATE_LORA
RWKV_GN_EPS = 64e-5
D_HEADS = 8
D_NOPE = 64
D_ROPE = 32
D_VDIM = 64
Q_LORA = 256
KV_LORA = 128
D_WIDTH = D_HEADS * D_VDIM
D_COLS = Q_LORA + KV_LORA + D_ROPE
ODD_IN = C_COLS + D_COLS
MLA_SCALE = (D_NOPE + D_ROPE) ** -0.5
ROPE_BASE = 10000.0
Q_BLOCK = 128
N_EXPERTS = 16
N_EXPERT_GROUPS = 4
EXPERTS_PER_GROUP = N_EXPERTS // N_EXPERT_GROUPS
TOP_K = 2
D_EXPERT = 256

kernel_name = 'hybrid_pool_sgu_rwkv7_mla_moe_step'

def _layernorm(x, g, b):
    xf = x.astype(F32)
    mu = xf.mean(-1, keepdims=True)
    var = jnp.mean(jnp.square(xf - mu), -1, keepdims=True)
    return ((xf - mu) * lax.rsqrt(var + LN_EPS) * g + b).astype(x.dtype)

def _rmsnorm(x, g):
    xf = x.astype(F32)
    return (xf * lax.rsqrt(jnp.mean(xf * xf, -1, keepdims=True) + RMS_EPS) * g).astype(x.dtype)

def _group_norm(x, n_groups, g, b, eps):
    xf = x.astype(F32).reshape(x.shape[:-1] + (n_groups, x.shape[-1] // n_groups))
    mu = xf.mean(-1, keepdims=True)
    var = jnp.mean(jnp.square(xf - mu), -1, keepdims=True)
    xn = ((xf - mu) * lax.rsqrt(var + eps)).reshape(x.shape)
    return (xn * g + b).astype(x.dtype)

def _rope(x, positions):
    half = x.shape[-1] // 2
    inv = ROPE_BASE ** (-jnp.arange(half, dtype=F32) / half)
    ang = (positions[:, None] * inv).reshape((positions.shape[0],) + (1,) * (x.ndim - 3) + (half,))
    cos, sin = jnp.cos(ang), jnp.sin(ang)
    xf = x.astype(F32)
    x1, x2 = xf[..., :half], xf[..., half:]
    return jnp.concatenate([x1 * cos - x2 * sin, x1 * sin + x2 * cos], -1).astype(x.dtype)

def _multi_scale_pool(a, start_pos):
    L = a.shape[1]
    af = a.astype(F32)
    cs = jnp.pad(jnp.cumsum(af, axis=1), ((0, 0), (1, 0), (0, 0)))
    pos = start_pos + jnp.arange(L)
    outs = []
    for g, w in enumerate(POOL_WINDOWS):
        sl = slice(g * A_GROUP_DIM, (g + 1) * A_GROUP_DIM)
        hi = cs[:, 1:, sl]
        lo = jnp.pad(cs[:, :L + 1 - w, sl], ((0, 0), (w - 1, 0), (0, 0)))
        cnt = jnp.minimum(w, pos + 1).astype(F32)
        outs.append((hi - lo) / cnt[None, :, None])
    return jnp.concatenate(outs, -1) - af

def _chunk_spatial_mix(v, w_s, b_s):
    B, L, _ = v.shape
    cl = min(L, CHUNK)
    n = -(-L // cl)
    vh = jnp.pad(v, ((0, 0), (0, n * cl - L), (0, 0))).reshape(B, n, cl, B_HEADS, B_HEAD_DIM)
    w = w_s[:, :cl, :cl] * jnp.tril(jnp.ones((cl, cl), w_s.dtype))
    mix = jnp.einsum('hij,bnjhc->bnihc', w, vh) + b_s[:, :cl].T[None, None, :, :, None]
    return mix.reshape(B, n * cl, B_WIDTH)[:, :L]

def _even_mixer(x, pool_buf, start_pos, w_in, pool_w, pool_scale, sgu_g, sgu_bn, sgu_w, sgu_b, w_out):
    B, L, _ = x.shape
    p = x @ w_in
    a = p[..., :A_WIDTH]
    z = jax.nn.gelu(p[..., A_WIDTH:], approximate=False)
    u, v = z[..., :B_WIDTH], z[..., B_WIDTH:]
    a_ext = a if pool_buf is None else jnp.concatenate([pool_buf.astype(a.dtype), a], axis=1)
    ext_start = start_pos - (a_ext.shape[1] - L)
    pooled = _multi_scale_pool(a_ext, ext_start)[:, -L:].reshape(B, L, A_GROUPS, A_GROUP_DIM)
    a_out = (jnp.einsum('blgc,gcd->blgd', pooled, pool_w).reshape(B, L, A_WIDTH) * pool_scale).astype(x.dtype)
    vn = _group_norm(v, B_HEADS, sgu_g, sgu_bn, LN_EPS)
    b_out = u * _chunk_spatial_mix(vn, sgu_w, sgu_b)
    y = jnp.concatenate([a_out, b_out], -1) @ w_out
    return y, a_ext[:, -POOL_BUF:], vn

def _rwkv7(pc, shift_in, S_in, mu, w0, w2, a0, a2, g2, kkc, kac, rk, gn_g, gn_b):
    B, L, _ = pc.shape
    prev = jnp.concatenate([shift_in.astype(pc.dtype), pc[:, :-1]], axis=1)
    xs = (pc + (prev - pc) * mu).astype(F32)
    C, o1, o2 = C_WIDTH, 3 * C_WIDTH + C_DECAY_LORA, 3 * C_WIDTH + C_DECAY_LORA + C_ICLR_LORA
    r, k, v = xs[..., :C], xs[..., C:2 * C], xs[..., 2 * C:3 * C]
    wl, al, gl = xs[..., 3 * C:o1], xs[..., o1:o2], xs[..., o2:]
    log_w = -jax.nn.softplus(-(w0 + jnp.tanh(wl) @ w2)) - 0.5
    decay = jnp.exp(-jnp.exp(log_w))
    a = jax.nn.sigmoid(a0 + al @ a2)
    g = jax.nn.sigmoid(gl) @ g2
    heads = lambda t: t.reshape(B, L, C_HEADS, C_HEAD_DIM)
    kk = heads(k * kkc)
    kk = kk * lax.rsqrt(jnp.sum(kk * kk, -1, keepdims=True) + 1e-12)
    k = k * (1.0 + (a - 1.0) * kac)
    rh, wh, kh, vh, ah = heads(r), heads(decay), heads(k), heads(v), heads(a)

    def step(S, inp):
        r_t, w_t, k_t, v_t, kk_t, a_t = inp
        sa = jnp.einsum('bhvk,bhk->bhv', S, kk_t)
        S = S * w_t[:, :, None, :] - sa[..., None] * (kk_t * a_t)[:, :, None, :] + v_t[..., None] * k_t[:, :, None, :]
        return S, jnp.einsum('bhvk,bhk->bhv', S, r_t)

    seq = tuple(jnp.moveaxis(t, 1, 0) for t in (rh, wh, kh, vh, kk, ah))
    S_out, y = lax.scan(step, S_in.astype(F32), seq)
    y = jnp.moveaxis(y, 0, 1).reshape(B, L, C)
    yn = _group_norm(y, C_HEADS, gn_g, gn_b, RWKV_GN_EPS)
    bonus = jnp.sum(rh * kh * rk.reshape(C_HEADS, C_HEAD_DIM), -1, keepdims=True) * vh
    out = (yn + bonus.reshape(B, L, C)) * g
    return out.astype(pc.dtype), S_out, pc[:, -1:]

def _mla_project(pd, positions, gq, gkv, wuq, wuk):
    B, L, _ = pd.shape
    cq = _rmsnorm(pd[..., :Q_LORA], gq)
    ckv = _rmsnorm(pd[..., Q_LORA:Q_LORA + KV_LORA], gkv)
    kpe = _rope(pd[..., Q_LORA + KV_LORA:], positions)
    q = (cq @ wuq).reshape(B, L, D_HEADS, D_NOPE + D_ROPE)
    q_pe = _rope(q[..., D_NOPE:], positions)
    q_lat = jnp.einsum('blhn,hcn->blhc', q[..., :D_NOPE], wuk)
    return q_lat, q_pe, ckv, kpe

def _mla_scores(q_lat, q_pe, ckv, kpe):
    s = jnp.einsum('bqhc,bkc->bhqk', q_lat.astype(F32), ckv.astype(F32))
    s = s + jnp.einsum('bqhr,bkr->bhqk', q_pe.astype(F32), kpe.astype(F32))
    return s * MLA_SCALE

def _online_update(carry, s, vals):
    m, l, acc = carry
    m_new = jnp.maximum(m, s.max(-1))
    corr = jnp.exp(m - m_new)
    p = jnp.exp(s - m_new[..., None])
    l = l * corr + p.sum(-1)
    acc = acc * corr[..., None] + jnp.einsum('bhqk,bkc->bhqc', p, vals.astype(F32))
    return (m_new, l, acc)

def _mla_attend_prompt(q_lat, q_pe, ckv, kpe):
    L = q_lat.shape[1]
    outs = []
    for s0 in range(0, L, Q_BLOCK):
        e = min(s0 + Q_BLOCK, L)
        s = _mla_scores(q_lat[:, s0:e], q_pe[:, s0:e], ckv[:, :e], kpe[:, :e])
        causal = jnp.arange(s0, e)[:, None] >= jnp.arange(e)[None, :]
        prob = jax.nn.softmax(jnp.where(causal, s, -jnp.inf), axis=-1)
        outs.append(jnp.einsum('bhqk,bkc->bqhc', prob, ckv[:, :e].astype(F32)))
    return jnp.concatenate(outs, axis=1)

def _mla_attend_paged(q_lat, q_pe, ckv, kpe, pool_ckv, pool_kpe, page_table):
    B, L = q_lat.shape[:2]

    def page_step(carry, pages):
        ck = pool_ckv[pages]
        kp = pool_kpe[pages]
        return _online_update(carry, _mla_scores(q_lat, q_pe, ck, kp), ck), None

    init = (jnp.full((B, D_HEADS, L), -jnp.inf, F32), jnp.zeros((B, D_HEADS, L), F32),
            jnp.zeros((B, D_HEADS, L, KV_LORA), F32))
    carry, _ = lax.scan(page_step, init, page_table.T)
    causal = jnp.arange(L)[:, None] >= jnp.arange(L)[None, :]
    s = jnp.where(causal, _mla_scores(q_lat, q_pe, ckv, kpe), -jnp.inf)
    m, l, acc = _online_update(carry, s, ckv)
    return jnp.moveaxis(acc / l[..., None], 1, 2)

def _odd_mixer(x, shift_in, S_in, positions, paged, w_in, mu, w0, w2, a0, a2, g2, kkc, kac, rk,
               gn_g, gn_b, gq, gkv, wuq, wuk, wuv, w_out):
    B, L, _ = x.shape
    p = x @ w_in
    y_c, S_out, shift_out = _rwkv7(p[..., :C_COLS], shift_in, S_in, mu, w0, w2, a0, a2, g2,
                                   kkc, kac, rk, gn_g, gn_b)
    q_lat, q_pe, ckv, kpe = _mla_project(p[..., C_COLS:], positions, gq, gkv, wuq, wuk)
    if paged is None:
        o_lat = _mla_attend_prompt(q_lat, q_pe, ckv, kpe)
    else:
        o_lat = _mla_attend_paged(q_lat, q_pe, ckv, kpe, paged[0], paged[1], paged[2])
    y_d = jnp.einsum('blhc,hcn->blhn', o_lat, wuv).reshape(B, L, D_WIDTH).astype(x.dtype)
    y = jnp.concatenate([y_c, y_d], -1) @ w_out
    return y, S_out, shift_out, ckv, kpe

def _moe(x, w_router, router_bias, w_gate, w_up, w_down):
    shape = x.shape
    h = x.reshape(-1, D_MODEL)
    T = h.shape[0]
    scores = jax.nn.sigmoid(h.astype(F32) @ w_router.astype(F32))
    biased = scores + router_bias.astype(F32)
    grp_top = lax.top_k(biased.reshape(T, N_EXPERT_GROUPS, EXPERTS_PER_GROUP), TOP_K)[0]
    group = jnp.argmax(grp_top.sum(-1), axis=-1)
    expert_group = jnp.arange(N_EXPERTS) // EXPERTS_PER_GROUP
    masked = jnp.where(expert_group[None, :] == group[:, None], biased, -jnp.inf)
    _, idx = lax.top_k(masked, TOP_K)
    wts = jnp.take_along_axis(scores, idx, axis=-1)
    wts = wts / wts.sum(-1, keepdims=True)
    gates = jnp.sum(jax.nn.one_hot(idx, N_EXPERTS, dtype=F32) * wts[..., None], axis=1).astype(h.dtype)
    y = jnp.zeros_like(h)
    for e in range(N_EXPERTS):
        he = jax.nn.silu(h @ w_gate[e]) * (h @ w_up[e])
        y = y + gates[:, e:e + 1] * (he @ w_down[e])
    return y.reshape(shape)

def setup_inputs(seed: int = 0) -> dict:
    key = jax.random.key(seed)
    keys = iter(jax.random.split(key, 48))

    def nrm(shape, scale):
        return jax.random.normal(next(keys), shape, F32) * scale

    def near_one(shape):
        return 1.0 + nrm(shape, 0.05)

    n_pages = PAST_LEN // PAGE_SIZE
    n_pool = (DEC_BATCH * n_pages * 5) // 4
    x_prompt = nrm((BATCH, SEQ, D_MODEL), 1.0)
    x_sample = nrm((DEC_BATCH, DEC_SEQ, D_MODEL), 1.0)
    state_pool_buf = nrm((N_EVEN, DEC_BATCH, POOL_BUF, A_WIDTH), 1.0)
    state_rwkv = nrm((N_ODD, DEC_BATCH, C_HEADS, C_HEAD_DIM, C_HEAD_DIM), 0.2)
    state_shift = nrm((N_ODD, DEC_BATCH, 1, C_COLS), 1.0)
    cache_ckv = nrm((N_ODD, n_pool, PAGE_SIZE, KV_LORA), 1.0)
    cache_kpe = nrm((N_ODD, n_pool, PAGE_SIZE, D_ROPE), 1.0)
    perm = jax.random.permutation(next(keys), n_pool)
    page_table = perm[:DEC_BATCH * n_pages].reshape(DEC_BATCH, n_pages).astype(jnp.int32)
    return {
        'x_prompt': x_prompt,
        'x_sample': x_sample,
        'state_pool_buf': state_pool_buf,
        'state_rwkv': state_rwkv,
        'state_shift': state_shift,
        'cache_ckv': cache_ckv,
        'cache_kpe': cache_kpe,
        'page_table': page_table,
        'ln_g': near_one((DEPTH, 2, D_MODEL)),
        'ln_b': nrm((DEPTH, 2, D_MODEL), 0.02),
        'w_in_even': nrm((N_EVEN, D_MODEL, EVEN_IN), D_MODEL ** -0.5),
        'pool_w': nrm((N_EVEN, A_GROUPS, A_GROUP_DIM, A_GROUP_DIM), A_GROUP_DIM ** -0.5),
        'pool_scale': near_one((N_EVEN, A_WIDTH)),
        'sgu_ln_g': near_one((N_EVEN, B_WIDTH)),
        'sgu_ln_b': nrm((N_EVEN, B_WIDTH), 0.02),
        'sgu_w': nrm((N_EVEN, B_HEADS, CHUNK, CHUNK), CHUNK ** -0.5),
        'sgu_b': near_one((N_EVEN, B_HEADS, CHUNK)),
        'w_out_even': nrm((N_EVEN, A_WIDTH + B_WIDTH, D_MODEL), BETA * (A_WIDTH + B_WIDTH) ** -0.5),
        'w_in_odd': nrm((N_ODD, D_MODEL, ODD_IN), D_MODEL ** -0.5),
        'rwkv_mu': jax.random.uniform(next(keys), (N_ODD, C_COLS), F32, 0.0, 1.0),
        'rwkv_w0': jax.random.uniform(next(keys), (N_ODD, C_WIDTH), F32, -3.0, 1.0),
        'rwkv_w2': nrm((N_ODD, C_DECAY_LORA, C_WIDTH), 0.1),
        'rwkv_a0': nrm((N_ODD, C_WIDTH), 0.1),
        'rwkv_a2': nrm((N_ODD, C_ICLR_LORA, C_WIDTH), C_ICLR_LORA ** -0.5),
        'rwkv_g2': nrm((N_ODD, C_GATE_LORA, C_WIDTH), C_GATE_LORA ** -0.5),
        'rwkv_kk': 0.85 + nrm((N_ODD, C_WIDTH), 0.05),
        'rwkv_ka': near_one((N_ODD, C_WIDTH)),
        'rwkv_rk': nrm((N_ODD, C_WIDTH), 0.1),
        'rwkv_gn_g': near_one((N_ODD, C_WIDTH)),
        'rwkv_gn_b': nrm((N_ODD, C_WIDTH), 0.02),
        'mla_gq': near_one((N_ODD, Q_LORA)),
        'mla_gkv': near_one((N_ODD, KV_LORA)),
        'mla_wuq': nrm((N_ODD, Q_LORA, D_HEADS * (D_NOPE + D_ROPE)), Q_LORA ** -0.5),
        'mla_wuk': nrm((N_ODD, D_HEADS, KV_LORA, D_NOPE), KV_LORA ** -0.5),
        'mla_wuv': nrm((N_ODD, D_HEADS, KV_LORA, D_VDIM), KV_LORA ** -0.5),
        'w_out_odd': nrm((N_ODD, C_WIDTH + D_WIDTH, D_MODEL), BETA * (C_WIDTH + D_WIDTH) ** -0.5),
        'w_router': nrm((D_MODEL, N_EXPERTS), D_MODEL ** -0.5),
        'router_bias': nrm((N_EXPERTS,), 0.01),
        'w_gate': nrm((DEPTH, N_EXPERTS, D_MODEL, D_EXPERT), D_MODEL ** -0.5),
        'w_up': nrm((DEPTH, N_EXPERTS, D_MODEL, D_EXPERT), D_MODEL ** -0.5),
        'w_down': nrm((DEPTH, N_EXPERTS, D_EXPERT, D_MODEL), BETA * D_EXPERT ** -0.5),
    }

def reference(x_prompt, x_sample, state_pool_buf, state_rwkv, state_shift, cache_ckv, cache_kpe, page_table,
              ln_g, ln_b, w_in_even, pool_w, pool_scale, sgu_ln_g, sgu_ln_b, sgu_w, sgu_b, w_out_even,
              w_in_odd, rwkv_mu, rwkv_w0, rwkv_w2, rwkv_a0, rwkv_a2, rwkv_g2, rwkv_kk, rwkv_ka, rwkv_rk,
              rwkv_gn_g, rwkv_gn_b, mla_gq, mla_gkv, mla_wuq, mla_wuk, mla_wuv, w_out_odd,
              w_router, router_bias, w_gate, w_up, w_down):
    past_len = page_table.shape[1] * PAGE_SIZE
    bp, lp = x_prompt.shape[:2]
    ls = x_sample.shape[1]
    pos_p = jnp.arange(lp, dtype=F32)
    pos_s = past_len + jnp.arange(ls, dtype=F32)
    xp, xs = x_prompt, x_sample
    pool_p, pool_s, sgu_s = [], [], []
    rwkv_p, rwkv_s, shift_p, shift_s = [], [], [], []
    ckv_p, ckv_s, kpe_p, kpe_s = [], [], [], []
    for layer in range(DEPTH):
        i = layer // 2
        if layer % 2 == 0:
            ew = (w_in_even[i], pool_w[i], pool_scale[i], sgu_ln_g[i], sgu_ln_b[i], sgu_w[i], sgu_b[i], w_out_even[i])
            yp, buf_p, _ = _even_mixer(xp, None, 0, *ew)
            ys, buf_s, v_s = _even_mixer(xs, state_pool_buf[i], past_len, *ew)
            pool_p.append(buf_p)
            pool_s.append(buf_s.astype(state_pool_buf.dtype))
            sgu_s.append(v_s)
        else:
            ow = (w_in_odd[i], rwkv_mu[i], rwkv_w0[i], rwkv_w2[i], rwkv_a0[i], rwkv_a2[i], rwkv_g2[i],
                  rwkv_kk[i], rwkv_ka[i], rwkv_rk[i], rwkv_gn_g[i], rwkv_gn_b[i], mla_gq[i], mla_gkv[i],
                  mla_wuq[i], mla_wuk[i], mla_wuv[i], w_out_odd[i])
            shift0 = jnp.zeros((bp, 1, C_COLS), xp.dtype)
            S0 = jnp.zeros((bp, C_HEADS, C_HEAD_DIM, C_HEAD_DIM), F32)
            yp, S_p, sh_p, c_p, k_p = _odd_mixer(xp, shift0, S0, pos_p, None, *ow)
            ys, S_s, sh_s, c_s, k_s = _odd_mixer(xs, state_shift[i], state_rwkv[i], pos_s,
                                                 (cache_ckv[i], cache_kpe[i], page_table), *ow)
            rwkv_p.append(S_p.astype(xp.dtype))
            rwkv_s.append(S_s.astype(state_rwkv.dtype))
            shift_p.append(sh_p)
            shift_s.append(sh_s.astype(state_shift.dtype))
            ckv_p.append(c_p)
            ckv_s.append(c_s.astype(cache_ckv.dtype))
            kpe_p.append(k_p)
            kpe_s.append(k_s.astype(cache_kpe.dtype))
        xp = _layernorm(ALPHA * xp + yp, ln_g[layer, 0], ln_b[layer, 0])
        xs = _layernorm(ALPHA * xs + ys, ln_g[layer, 0], ln_b[layer, 0])
        xp = _layernorm(ALPHA * xp + _moe(xp, w_router, router_bias, w_gate[layer], w_up[layer], w_down[layer]),
                        ln_g[layer, 1], ln_b[layer, 1])
        xs = _layernorm(ALPHA * xs + _moe(xs, w_router, router_bias, w_gate[layer], w_up[layer], w_down[layer]),
                        ln_g[layer, 1], ln_b[layer, 1])
    pool_buf_prompt = jnp.stack(pool_p)
    pool_buf_sample = jnp.stack(pool_s)
    sgu_v_sample = jnp.stack(sgu_s)
    rwkv_state_prompt = jnp.stack(rwkv_p)
    rwkv_state_sample = jnp.stack(rwkv_s)
    shift_prompt = jnp.stack(shift_p)
    shift_sample = jnp.stack(shift_s)
    ckv_prompt = jnp.stack(ckv_p)
    ckv_sample = jnp.stack(ckv_s)
    kpe_prompt = jnp.stack(kpe_p)
    kpe_sample = jnp.stack(kpe_s)
    return (xp, xs, pool_buf_prompt, pool_buf_sample, sgu_v_sample, rwkv_state_prompt, rwkv_state_sample,
            shift_prompt, shift_sample, ckv_prompt, ckv_sample, kpe_prompt, kpe_sample)


_drawn_inputs = setup_inputs


def setup_inputs(seed=0):
    import zlib

    import numpy as np

    out = dict(_drawn_inputs(seed))
    spreads = {}
    factors = {'cache_ckv': 3.63,
     'cache_kpe': 8.0,
     'sgu_ln_b': 3.017,
     'rwkv_kk': 3.246,
     'rwkv_gn_g': 3.855,
     'rwkv_gn_b': 6.04,
     'mla_gq': 6.953}
    for name, (base, spread) in spreads.items():
        noise = np.random.default_rng([zlib.crc32(name.encode()), seed]).standard_normal(out[name].shape)
        drawn = base * np.exp(spread * noise) if base else spread * noise
        out[name] = __import__('jax').numpy.asarray(drawn.astype(out[name].dtype))
    for name, factor in factors.items():
        out[name] = (out[name] * factor).astype(out[name].dtype)
    return out
```

```python
from contextlib import ExitStack

import numpy as np
import concourse.bass as bass
from concourse import mybir

ALU = mybir.AluOpType
ACT = mybir.ActivationFunctionType
AX = mybir.AxisListType
F32 = mybir.dt.float32

P = 128
D_MODEL = 1024
KC = D_MODEL // P
SEQ = 512
DEC_B, DEC_T = 8, 8
NS = DEC_B * DEC_T
T = SEQ + NS
ROWS = [P] * (SEQ // P) + [NS]
NT = len(ROWS)
SPLITS = [(0, SEQ), (SEQ, NS)]
DEPTH = 2
ALPHA = (2 * DEPTH) ** 0.25
LN_EPS, RMS_EPS, GN_EPS = 1e-5, 1e-6, 64e-5
WINDOWS = (2, 4, 8, 16)
POOL_BUF = 15
A_W = 512
EVEN_IN = 1536
HB = 4
C_COLS = 1792
CT = C_COLS // P
ODD_IN = 2208
Q_LORA, KV_LORA, D_ROPE, D_NOPE = 256, 128, 32, 64
D_COLS = Q_LORA + KV_LORA + D_ROPE
NH = 8
HD = 64
MLA_SCALE = (D_NOPE + D_ROPE) ** -0.5
PAST = 2048
PAGE = 128
NPG = PAST // PAGE
N_EXP, EPG, NG = 16, 4, 4
D_EXP = 256
DECAY = float(np.exp(-0.5))
CH = 64
SUB = 16

NBANK = 8
BIG = 1e30
SLOT = 2048
NSLOT = 5


def constant_table():
    cols = {}
    parts = []
    at = 0

    def put(name, a):
        nonlocal at
        full = np.zeros((P, a.shape[1]), np.float32)
        full[:a.shape[0]] = a
        cols[name] = (at, a.shape[1])
        at += a.shape[1]
        parts.append(full)

    i = np.arange(P)[:, None]
    t = np.arange(P)[None, :]
    chunk = i // CH == t // CH
    sub = i // SUB == t // SUB
    put("ident", np.eye(P))
    put("lane", i % D_ROPE * 1.0)
    put("mNd", sub & (i < t))
    put("mNo", chunk & ~sub & (i < t))
    put("mG2", chunk & (i < t))
    put("mG3", -1.0 * (chunk & (i <= t)))
    put("mG4", chunk & (i <= t))
    put("mMd", sub & (i > t))
    put("cum", np.concatenate([chunk & (i <= t), chunk & (i < t)], 1))
    put("triu", i <= t)
    put("negtri", np.where(t <= i, 0.0, -BIG))
    put("before", i < t)
    put("ones", np.ones((P, P)))
    put("rowbase", np.tile(P * np.arange(N_EXP) * 1.0, (P, 1)))
    i = np.arange(NS)[:, None]
    t = np.arange(NS)[None, :]
    same = i // DEC_T == t // DEC_T
    put("sNd", same & (i < t))
    put("sG3", -1.0 * (same & (i <= t)))
    put("sG4", same & (i <= t))
    put("sMd", same & (i > t))
    put("scum", np.concatenate([same & (i <= t), same & (i < t)], 1))
    put("ofbatch", i // DEC_T == np.arange(DEC_B)[None, :])
    q = np.arange(NS)[:, None] % DEC_T
    b, k = np.arange(DEC_B)[None, :, None], np.arange(NS)[None, None, :]
    seen = (k // DEC_T == b) & (k % DEC_T <= q[:, :, None])
    put("negS", np.where(seen, 0.0, -BIG).reshape(NS, -1))
    corr = np.ones((P, HB, 16))
    for g, w in enumerate(WINDOWS):
        corr[:, g] = (w / np.minimum(w, np.arange(16) + 1.0))[None]
    put("corr", corr.reshape(P, -1))
    put("iota", np.tile(np.arange(N_EXP) - float(N_EXP), (P, 1)))
    put("headof", (np.arange(P)[:, None] // HD == np.arange(P)[None, :] // HD) * 1.0)
    pos = np.concatenate([np.arange(SEQ), PAST + np.tile(np.arange(DEC_T), DEC_B)]).astype(np.float32)
    half = D_ROPE // 2
    inv = (np.float32(10000.0) ** (-np.arange(half, dtype=np.float32) / np.float32(half))).astype(np.float32)
    ang = (pos[:, None] * inv).astype(np.float32)
    cos, sin = np.cos(ang), np.sin(ang)
    pad = np.zeros((NT * P - T, half))
    put("cos", np.concatenate([cos, pad]).reshape(NT, P, half).transpose(1, 0, 2).reshape(P, -1))
    put("sin", np.concatenate([sin, pad]).reshape(NT, P, half).transpose(1, 0, 2).reshape(P, -1))
    rows = np.arange(P) % D_ROPE
    put("cosT", cos.T[rows % half])
    put("sinT", sin.T[rows % half] * np.where(rows < half, -1.0, 1.0)[:, None])
    return np.concatenate(parts, 1).astype(np.float32), cols


CONST, CCOL = constant_table()


LAYERS = 2


JOBS = {}
N_JOBS = 0


def reserve(name, n=1):
    global N_JOBS
    JOBS[name] = (N_JOBS, n)
    N_JOBS += n


STEPS = ["MT", "M", "G3", "G2", "G4", "N2", "M2", "N4", "M4", "M8", "X1", "X2", "X3", "Y", "HT", "H", "H2T", "Z",
         "TT", "G2V", "U", "WT"]
STEPS_S = ["MT", "M", "G3", "G2", "G4", "N2", "M2", "M4", "X1", "X2", "G2V", "U", "WT"]
N_ATT = NH * (SEQ // P)
LAG = 2

for layer in range(LAYERS):
    L = f"{layer}."
    if layer % 2 == 0:
        reserve("au", 16)
        reserve("v", NT)
        reserve("pool", 2 * HB)
        reserve("mix", NT)
    else:
        reserve("xT", 2 * NT)
        reserve("c", 2 * CT)
        reserve("dtok", NT)
        reserve("decay", NT)
        reserve("iclr", 2 * HB)
        reserve("norm", 2 * HB)
        reserve("dT", NT)
        reserve("bonus")
        reserve("cum", 2 * NT)
        for tile in range(NT):
            reserve(f"tok{tile}", 4)
            reserve(f"unit{tile}", 2 * len(STEPS if tile < NT - 1 else STEPS_S))
            if tile < NT - 1:
                reserve(f"chain{tile}", 6)
            else:
                reserve("schain", 3 * NH)
            reserve(f"y{tile}", 2)
            reserve(f"yT{tile}")
        reserve("qpe", 8)
        reserve("q0a", 2)
        reserve("q0b", 2)
        for u in range(N_ATT + LAG + 2):
            if u < N_ATT:
                reserve(f"S{u}")
                if u % 4 in (1, 2) and u + 4 < N_ATT:
                    reserve(f"q{u // 4 + 1}{'ab'[u % 4 - 1]}", 2)
            if 0 <= u - LAG < N_ATT:
                reserve(f"PT{u - LAG}")
            if 0 <= u - LAG - 1 < N_ATT:
                reserve(f"O{u - LAG - 1}")
            if u - LAG - 2 >= 0 and (u - LAG - 2) % 4 == 3:
                reserve(f"yd{(u - LAG - 2) // 4}")
        reserve("own")
        for b in range(DEC_B + 1):
            if b < DEC_B:
                reserve(f"Sb{b}l", 3)
            if b > 0:
                reserve(f"PTb{b - 1}", 3)
            if b < DEC_B:
                reserve(f"Sb{b}h")
            if b > 0:
                reserve(f"Ob{b - 1}")
        reserve("ydS")
    reserve(L + "out", 2 * NT)
    reserve(L + "mT", 2 * NT)
    reserve(L + "router")
    reserve(L + "pos")
    for e in range(N_EXP):
        reserve(f"{L}e{e}", 8 + 2 * NT)


def job(name, i=0):
    first, n = JOBS[name]
    assert 0 <= i < n, (name, i)
    return first + i


SPARSE = ["T0", "T1", "GU", "HT", "D0", "D1"]
SPARSE_ORDER = {}
for kind in ("T0", "T1"):
    SPARSE_ORDER[0, kind] = len(SPARSE_ORDER)
for e in range(N_EXP + 1):
    for at, kind in ((e + 1, "T0"), (e + 1, "T1"), (e - 1, "HT"), (e, "GU"), (e - 1, "D0"), (e - 1, "D1")):
        if 0 <= at < N_EXP:
            SPARSE_ORDER[at, kind] = len(SPARSE_ORDER)


def sparse_job(layer, e, kind):
    return job(f"{layer}.e0") + SPARSE_ORDER[e, kind]


def state_job(h, k):
    if k < 2:
        return job("schain", k if h == 0 else 3 * h - 1 + k)
    return job("schain", min(3 * h + 4, 3 * NH - 1))


def batch_job(b, g):
    return job(f"Sb{b}l", g) if g < 3 else job(f"Sb{b}h", g - 3)


def unit_job(tile, step, parity):
    return job(f"unit{tile}", 2 * (STEPS if tile < NT - 1 else STEPS_S).index(step) + parity)


NSPARSE = NSLOT + 6
NXG = 4
NYS = 3
SP_PAGES = 11
NPGB = 3


BLOCKS = []
FIRST_EXPERT_BLOCK = []
BLOCK_AT = {}


def block(key, last_job):
    BLOCK_AT[key] = len(BLOCKS)
    BLOCKS.append((key, last_job))


for n in range(6):
    block(("ein", n), job("au", 4 * n + 3) if n < 4 else job("v", NT - 1))
for layer in range(LAYERS):
    if layer == 1:
        for n in range(9):
            block(("oin", n), job("c", 4 * n + 3) if n < 7 else job("dtok", NT - 1))
        for n in range(NSLOT):
            block(("scratch", n), job("ydS"))
    for n in range(4):
        block(("wout", layer, n), job(f"{layer}.out", NT * (n // 2) + NT - 1))
    for e in range(N_EXP):
        if e == 0:
            FIRST_EXPERT_BLOCK.append(len(BLOCKS))
        for q in range(2):
            block(("w_gu", layer, e, q), job(f"{layer}.e{e}", 7))
        block(("w_down", layer, e), job(f"{layer}.e{e}", 7 + 2 * NT))
LOADED = [n for n, (key, _) in enumerate(BLOCKS) if key[0] != "scratch"]
ROW_AT = {n: i for i, n in enumerate(LOADED)}


def columns(spec):
    at, out = 0, {}
    for name, n in spec:
        out[name] = (at, n)
        at += n
    return out, at


EV, EV_W = columns([("poolw", 512), ("pscale", 4), ("sguT", 512), ("sguTs", HB * NS), ("sbias", 512),
                    ("sbiasS", HB * NS), ("sgg", 512), ("sgb", 512)])
RW, RW_W = columns([("mu", CT), ("a0", 4), ("kkc", 4), ("kac", 4), ("rk", 32), ("w2a2", 512), ("g2", 512),
                    ("w0", 512), ("gng", 512), ("gnb", 512), ("shift", CT * DEC_B), ("gq", 256), ("gkv", 128)])
ML, ML_W = columns([("wuqn", 1024), ("wuqp", 512), ("wuqs", 512), ("wukT", 1024), ("wuv", 512)])


def pack(spec, width, parts):
    out = np.zeros((P, width), np.float32)
    for name, a in parts.items():
        at, n = spec[name]
        out[:a.shape[0], at:at + n] = np.asarray(a).reshape(a.shape[0], n)
    return out


def lay_out(i):
    f = lambda name: np.asarray(i[name])
    rep = lambda a: np.broadcast_to(a.reshape(1, -1), (P, a.size))
    colsof = lambda a: a.reshape(-1, P).T

    def chunks(w):
        return w.reshape(-1, P, w.shape[1]).transpose(1, 0, 2)

    stream = np.zeros((len(LOADED), P, SLOT), np.float32)
    for r, n in enumerate(LOADED):
        kind, *rest = BLOCKS[n][0]
        if kind in ("ein", "oin"):
            w = chunks(f("w_in_even" if kind == "ein" else "w_in_odd")[0][:, 256 * rest[0]:256 * rest[0] + 256])
            stream[r].reshape(P, KC, 256)[:, :, 0:w.shape[2]] = w
        elif kind == "wout":
            w = f("w_out_even" if rest[0] == 0 else "w_out_odd")[0]
            stream[r] = chunks(w[:, 256 * rest[1]:256 * rest[1] + 256]).reshape(P, SLOT)
        elif kind == "w_gu":
            both = [chunks(f(k)[rest[0], rest[1]])[:, 4 * rest[2]:4 * rest[2] + 4] for k in ("w_gate", "w_up")]
            stream[r] = np.concatenate(both, 2).reshape(P, SLOT)
        else:
            stream[r] = chunks(f(kind)[rest[0], rest[1]]).reshape(P, SLOT)

    xs = f("x_sample").reshape(NS, D_MODEL)
    xp = f("x_prompt")[0]
    x = np.zeros((P, NT, D_MODEL), np.float32)
    x[:, 0:4] = xp.reshape(4, P, D_MODEL).transpose(1, 0, 2)
    x[0:NS, 4] = xs
    xT = np.concatenate([xp, xs]).T.reshape(KC, P, T).transpose(1, 0, 2).reshape(P, -1)

    sgu = f("sgu_w")[0]
    sguTs = np.zeros((NS, HB, NS), np.float32)
    sbS = np.zeros((HB, DEC_B, DEC_T), np.float32)
    sbS[:] = f("sgu_b")[0][:, None, 0:DEC_T]
    for b in range(DEC_B):
        q = slice(DEC_T * b, DEC_T * b + DEC_T)
        sguTs[q, :, q] = sgu[:, 0:DEC_T, 0:DEC_T].transpose(2, 0, 1)
    even = pack(EV, EV_W, {
        "poolw": f("pool_w")[0].transpose(1, 0, 2), "pscale": colsof(f("pool_scale")[0]),
        "sguT": sgu.transpose(2, 0, 1), "sguTs": sguTs, "sbias": rep(f("sgu_b")[0]), "sbiasS": rep(sbS),
        "sgg": rep(f("sgu_ln_g")[0]), "sgb": rep(f("sgu_ln_b")[0])})
    buf = f("state_pool_buf")[0].reshape(DEC_B, POOL_BUF, HB, P).transpose(3, 2, 0, 1).reshape(P, -1)

    rk = np.zeros((P, 4, NH), np.float32)
    for h in range(NH):
        rk[HD * (h % 2):HD * (h % 2) + HD, h // 2, h] = f("rwkv_rk")[0, HD * h:HD * h + HD]
    rwkv = pack(RW, RW_W, {
        "mu": colsof(f("rwkv_mu")[0]), "a0": colsof(f("rwkv_a0")[0]), "kkc": colsof(f("rwkv_kk")[0]),
        "kac": colsof(f("rwkv_ka")[0]), "rk": rk, "w2a2": np.concatenate([f("rwkv_w2")[0], f("rwkv_a2")[0]]),
        "g2": f("rwkv_g2")[0], "w0": rep(f("rwkv_w0")[0]), "gng": rep(f("rwkv_gn_g")[0]),
        "gnb": rep(f("rwkv_gn_b")[0]),
        "shift": f("state_shift")[0, :, 0].reshape(DEC_B, CT, P).transpose(2, 1, 0),
        "gq": rep(f("mla_gq")[0]), "gkv": rep(f("mla_gkv")[0])})
    state = f("state_rwkv")[0].reshape(DEC_B, 4, 2, HD, HD).transpose(2, 4, 1, 0, 3).reshape(P, -1)

    wuq = f("mla_wuq")[0].reshape(2, P, NH, D_NOPE + D_ROPE).transpose(1, 0, 2, 3)
    pe = wuq[..., D_NOPE:]
    swapped = np.concatenate([pe[..., D_ROPE // 2:], pe[..., :D_ROPE // 2]], -1)
    mla = pack(ML, ML_W, {
        "wuqn": wuq[..., :D_NOPE], "wuqp": pe, "wuqs": swapped,
        "wukT": f("mla_wuk")[0].transpose(2, 0, 1), "wuv": f("mla_wuv")[0].transpose(1, 0, 2)})
    ck = f("cache_ckv")[0]
    pages = np.concatenate([ck.transpose(0, 2, 1), ck], 2)
    return {
        "const": CONST, "stream": stream, "x": x.reshape(P, -1), "xT": xT, "even": even, "buf": buf,
        "ln": np.concatenate([f("ln_g").reshape(4, -1), f("ln_b").reshape(4, -1)], 1),
        "wr": chunks(f("w_router")).reshape(P, -1), "rbias": rep(f("router_bias")),
        "rwkv": rwkv, "state": state, "mla": mla, "pages": pages,
        "pages_kpe": f("cache_kpe")[0].transpose(0, 2, 1), "table": f("page_table").reshape(1, -1),
        "table_kpe": np.repeat(f("page_table").reshape(DEC_B, 4, 4).transpose(1, 0, 2).reshape(4, -1), 32, axis=0)}


OUTS = {"x": (P, NT * D_MODEL), "pool_p": (P, HB * POOL_BUF), "pool_s": (P, HB * DEC_B * POOL_BUF),
        "sgu": (NS, 512), "state_p": (P, 4 * HD), "state_s": (P, 4 * DEC_B * HD), "shift": (P, CT * 9),
        "ckv": (P, NT * KV_LORA), "kpe": (P, NT * D_ROPE)}


def lay_back(o):
    x = o["x"].reshape(P, NT, D_MODEL)
    tok = lambda a: a.reshape(P, NT, -1)
    prompt = lambda a: tok(a)[:, 0:4].transpose(1, 0, 2).reshape(1, SEQ, -1)
    sample = lambda a: tok(a)[0:NS, 4].reshape(DEC_B, DEC_T, -1)
    pool_p = o["pool_p"].reshape(P, HB, POOL_BUF).transpose(2, 1, 0).reshape(1, 1, POOL_BUF, A_W)
    pool_s = o["pool_s"].reshape(P, HB, DEC_B, POOL_BUF).transpose(2, 3, 1, 0).reshape(1, DEC_B, POOL_BUF, A_W)
    st_p = o["state_p"].reshape(2, HD, 4, HD).transpose(2, 0, 3, 1).reshape(1, 1, NH, HD, HD)
    st_s = o["state_s"].reshape(2, HD, 4, DEC_B, HD).transpose(3, 2, 0, 4, 1).reshape(1, DEC_B, NH, HD, HD)
    sh = o["shift"].reshape(P, CT, 9).transpose(2, 1, 0).reshape(9, C_COLS)
    return (prompt(o["x"]), sample(o["x"]), pool_p, pool_s, o["sgu"].reshape(1, DEC_B, DEC_T, 512), st_p, st_s,
            sh[0:1].reshape(1, 1, 1, C_COLS), sh[1:].reshape(1, DEC_B, 1, C_COLS),
            prompt(o["ckv"])[None], sample(o["ckv"])[None], prompt(o["kpe"])[None], sample(o["kpe"])[None])


def program(nc, A, outs):
    ctx = ExitStack()
    with ctx:
        def sb(name, cols, rows=P):
            return ctx.enter_context(nc.sbuf_tensor(name, [rows, cols], F32))

        def sem(name):
            return ctx.enter_context(nc.semaphore(name))

        banks = [ctx.enter_context(nc.psum_tensor(f"bank{b}", [P, 512], F32)) for b in range(NBANK)]
        const = sb("const", CONST.shape[1])
        x_t = sb("x", NT * D_MODEL)
        acc_t = sb("acc", NT * D_MODEL)
        xT_t = sb("xT", KC * T)
        cat_t = sb("cat", KC * T)
        ring = sb("ring", NSLOT * SLOT)
        lnp = sb("lnp", 2 * D_MODEL)
        stat = sb("stat", 512)
        router = sb("router", (KC + 1) * N_EXP)
        WORK = 16450
        work = sb("work", WORK)

        def view(t, at, *shape):
            n = int(np.prod(shape))
            v = t[:, at:at + n]
            names = "abcd"[:len(shape)]
            if len(shape) > 1:
                v = v.rearrange(f"p ({' '.join(names)}) -> p {' '.join(names)}", **dict(zip(names, shape)))
            return v

        x = view(x_t, 0, NT, D_MODEL)
        acc = view(acc_t, 0, NT, D_MODEL)
        xT = view(xT_t, 0, KC, T)
        cat = view(cat_t, 0, KC, T)

        def c(name, rows=P):
            at, n = CCOL[name]
            return const[0:rows, at:at + n]

        def slot(n, *shape):
            return view(ring, (n % NSLOT) * SLOT, *shape)

        ident = c("ident")
        bn6 = view(stat, 0, NT, 2, 6)
        mv = view(stat, 64, NT, 2)
        rstd = view(stat, 80, NT)
        nmr = view(stat, 88, NT)

        filled = [sem(f"filled{b}") for b in range(NBANK)]
        emptied = [sem(f"emptied{b}") for b in range(NBANK)]
        slot_loaded = [sem(f"slot_loaded{s}") for s in range(NSLOT)]
        const_loaded = sem("const_loaded")
        x_loaded = sem("x_loaded")
        xT_loaded = sem("xT_loaded")
        even_loaded = sem("even_loaded")
        buf_loaded = sem("buf_loaded")
        buf_in_place = sem("buf_in_place")
        mask_applied = sem("mask_applied")
        router_loaded = sem("router_loaded")
        ln_loaded = sem("ln_loaded")
        cleared = sem("cleared")
        dve_step = sem("dve_step")
        act_step = sem("act_step")
        ln_stats = sem("ln_stats")
        ln_var = sem("ln_var")
        ln_std = sem("ln_std")
        ln_affine = sem("ln_affine")
        ln_scaled = sem("ln_scaled")
        ln_done = sem("ln_done")
        stored = sem("stored")
        pooled_ready = sem("pooled_ready")
        vn_var = sem("vn_var")
        vn_std = sem("vn_std")
        vn_ready = sem("vn_ready")
        gates_ready = sem("gates_ready")
        sel_ready = sem("sel_ready")
        rows_ready = sem("rows_ready")
        rows_cleared = sem("rows_cleared")
        scattered = [sem(f"scattered{k}") for k in range(LAYERS)]
        xg_loaded = [[sem(f"xg_loaded{k}{i}") for i in range(NXG)] for k in range(LAYERS)]
        spare_loaded = [[sem(f"spare_loaded{k}{i}") for i in range(NSPARSE)] for k in range(LAYERS)]
        silu_done = [sem(f"silu_done{k}") for k in range(LAYERS)]
        y_stored = [[sem(f"y_stored{k}{i}") for i in range(NYS)] for k in range(LAYERS)]
        combined = [sem(f"combined{k}") for k in range(LAYERS)]
        gathered = [[sem(f"gathered{k}{i}") for i in range(NT)] for k in range(LAYERS)]

        rwkv_loaded = sem("rwkv_loaded")
        state_loaded = sem("state_loaded")
        table_loaded = sem("table_loaded")
        kpe_rows = sem("kpe_rows")
        mla_loaded = sem("mla_loaded")
        page_loaded = [sem(f"page_loaded{i}") for i in range(NPGB)]
        gathered_pages = [sem(f"gathered_pages{i}") for i in range(NPGB)]
        state_stored = sem("state_stored")
        pc_begun = sem("pc_begun")
        xs_ready = sem("xs_ready")
        gate_in = sem("gate_in")
        rms_sum = sem("rms_sum")
        rms_std = sem("rms_std")
        mla_rows = sem("mla_rows")
        ld_ready = sem("ld_ready")
        sq_ready = sem("sq_ready")
        bonus_in = sem("bonus_in")
        kk_sum = sem("kk_sum")
        kk_std = sem("kk_std")
        scaled_ready = sem("scaled_ready")
        x0_ready = sem("x0_ready")
        state_reset = sem("state_reset")
        psel_ready = sem("psel_ready")
        gn_var = sem("gn_var")
        gn_std = sem("gn_std")
        qpe_ready = sem("qpe_ready")
        groups_ready = sem("groups_ready")
        smax = sem("smax")
        snorm = sem("snorm")
        smax_s = sem("smax_s")
        snorm_s = sem("snorm_s")
        n_stores = [0]

        def bank(n, *shape):
            b = banks[n % NBANK]
            if not shape:
                return b[:, :]
            m = int(np.prod(shape))
            names = "abcd"[:len(shape)]
            v = b[:, 0:m]
            if len(shape) > 1:
                v = v.rearrange(f"p ({' '.join(names)}) -> p {' '.join(names)}", **dict(zip(names, shape)))
            return v

        def claim(pe, n):
            if n >= NBANK:
                pe.wait_ge(emptied[n % NBANK], n // NBANK)

        def done(ins, n):
            ins.then_inc(filled[n % NBANK], 1)

        def take(eng, n):
            eng.wait_ge(filled[n % NBANK], n // NBANK + 1)

        def give(ins, n):
            ins.then_inc(emptied[n % NBANK], 1)

        def landed(eng, first, count):
            for n in range(max(first, first + count - NBANK), first + count):
                eng.wait_ge(emptied[n % NBANK], n // NBANK + 1)

        def landed_all(eng, name):
            landed(eng, *JOBS[name])

        def ejob(layer, e, kind):
            return sparse_job(layer, e, kind)

        def sparse_slot(layer, j, *shape):
            if j % NSPARSE < NSLOT:
                return slot(FIRST_EXPERT_BLOCK[layer] + j % NSPARSE, *shape)
            t = spare[j % NSPARSE - NSLOT]
            return view(t, 0, *shape)

        def sparse_weights(pe, layer, j):
            if j < NSLOT:
                weights(pe, BLOCKS[FIRST_EXPERT_BLOCK[layer] + j][0])
            else:
                pe.wait_ge(spare_loaded[layer][j % NSPARSE], 16 * (j // NSPARSE + (j % NSPARSE >= NSLOT)))

        def is_crowded(eng, layer):
            eng.wait_ge(rows_ready, layer + 1)
            return eng.value_load(crowded[0:1, 0:1], min_val=0, max_val=1)

        def weights(pe, key):
            n = BLOCK_AT[key]
            loads = sum(1 for m in LOADED if m <= n and m % NSLOT == n % NSLOT)
            pe.wait_ge(slot_loaded[n % NSLOT], 16 * loads)
            return n

        def stepper(eng, s):
            count = [0]

            def step(ins):
                count[0] += 1
                ins.then_inc(s, 1)
                eng.wait_ge(s, count[0])
            return step

        uT = view(work, 0, HB, T)
        aP = view(work, 2304, HB, 16 + SEQ)
        aS = view(work, 2304 + 2112, HB, DEC_B, POOL_BUF + DEC_T)
        o = 2304 + 2112 + 736
        vn = view(work, o, NT, A_W)
        o += NT * A_W
        sumP = view(work, o, 2, 16 + SEQ)
        o += 2 * (16 + SEQ)
        sumS = view(work, o, 2, DEC_B, POOL_BUF + DEC_T)
        o += 2 * DEC_B * (POOL_BUF + DEC_T)
        even = work[:, o:o + EV_W]
        even_at = o
        o += EV_W
        vstat = view(work, o, NT, HB, 6)
        o += NT * HB * 6
        vmv = view(work, o, NT, HB, 2)
        o += NT * HB * 2
        vrstd = view(work, o, NT, HB)
        o += NT * HB
        assert o <= WORK, o

        def ev(name, *shape):
            return view(work, even_at + EV[name][0], *shape)

        poolw, pscale = ev("poolw", HB, P), ev("pscale", HB)
        WT, WTs = ev("sguT", HB, P), ev("sguTs", HB, NS)
        sbias, sbiasS = ev("sbias", HB, P), ev("sbiasS", HB, NS)
        sgg, sgb = ev("sgg", A_W), ev("sgb", A_W)
        bufT = view(acc_t, 0, HB, DEC_B, POOL_BUF)
        pooled = view(acc_t, 512, HB, T)

        wr = view(router, 0, KC, N_EXP)
        rbias = view(router, KC * N_EXP, N_EXP)
        hT = view(work, 0, 2, 2, T)
        hg = view(work, 2304, 2, 2, T)
        o = 4608
        g_ = []
        for _ in range(7):
            g_.append(view(work, o, NT, N_EXP))
            o += NT * N_EXP
        score, biased, t0, t1, sel, both, gates = g_
        gs, gt, gm = (view(work, o + NT * NG * i, NT, NG) for i in range(3))
        o += 3 * NT * NG
        s1 = view(work, o, NT)
        s2 = view(work, o + NT, NT)
        row = view(work, o + 2 * NT, NT, 2)
        gate2 = view(work, o + 4 * NT, NT, 2)
        total = view(work, o + 6 * NT, N_EXP)
        o += 6 * NT + N_EXP
        assert o <= 5600, o
        o = 5600
        yg = view(work, o, NT, 2, D_MODEL)
        xg = view(work, o, NXG, D_MODEL)
        o += NXG * D_MODEL
        xgT = view(work, o, 2, KC, P)
        o += 2 * D_MODEL
        yS = view(work, o, NYS, D_MODEL)
        o += NYS * D_MODEL
        hgS = view(work, o, D_EXP)
        hS = view(work, o + D_EXP, 2, D_EXP)
        hTS = view(work, o + 3 * D_EXP, 2, 2, P)
        o += 5 * D_EXP
        assert o <= WORK, o
        spare = [t[:, SLOT * i:SLOT * i + SLOT] for t in (cat_t, xT_t, work) for i in range(2)]
        zero = work[:, WORK - D_MODEL - 16:WORK - 16]
        rowi = ctx.enter_context(nc.sbuf_tensor("rowi", [P, NT * 2], mybir.dt.int32))
        crowded = ctx.enter_context(nc.sbuf_tensor("crowded", [1, 1], mybir.dt.int32))
        xrows = nc.dram_tensor("xrows", [N_EXP * P, D_MODEL], F32).ap()
        yrows = nc.dram_tensor("yrows", [N_EXP * P, D_MODEL], F32).ap()


        o = 0
        rw_at = o
        o += RW_W
        stateS = view(work, o, 4, DEC_B, HD)
        o += 4 * DEC_B * HD
        stateP = view(work, o, 4, HD)
        o += 4 * HD
        cqT = view(work, o, 2, T)
        o += 2 * T
        ckvT = view(work, o, T)
        o += T
        kpeT = view(work, o, T)
        o += T
        ckv = view(work, o, NT, KV_LORA)
        o += NT * KV_LORA
        xs_at = o
        xs = view(work, o, CT, T)
        o += CT * T
        assert o <= WORK, o
        p_sb = view(cat_t, 3200, 4, 2, HD)
        y_sb = view(cat_t, 3712, 4, 2, HD)
        dec = view(stat, 128, 4, 2 * 4)
        decS = view(stat, 160, 4, DEC_B)
        ss = view(stat, 192, NT, 2)
        srs = view(stat, 202, NT, 2)
        okac = view(stat, 212, 4)
        shout = view(stat, 216, CT, 9)
        gn6 = view(stat, 342, NH, 6)
        gmv = view(stat, 390, NH, 2)
        grs = view(stat, 406, NH)
        bon = view(stat, 414, NT, NH)
        rinv = view(stat, 454, 4)
        rmax = view(stat, 458, 4)
        rsum = view(stat, 462, 4)
        alpha = view(xT_t, 0, 4, T)
        beta = view(xT_t, 4 * T, 4, T)
        kappa = view(acc_t, 0, 4, T)
        rho = view(acc_t, 4 * T, 4, T)
        pc = view(cat_t, 0, 2, 1 + SEQ + DEC_B * (1 + DEC_T))
        PCW = 1 + SEQ + DEC_B * (1 + DEC_T)
        pd = view(acc_t, 0, NT, D_COLS)
        ld = view(cat_t, 0, NT, A_W)
        kp4 = view(cat_t, 2560, NT, 4, D_ROPE)
        rtmp = view(lnp, 0, 2, NT, D_ROPE // 2)
        junk = view(lnp, 1000, 2, 256)
        expo = view(lnp, 0, 2, 3, 2, P)
        tokm = view(lnp, 0, 4, 4, 2, HD)

        def rw(name, *shape, rows=slice(0, P)):
            return view(work, rw_at + RW[name][0], *shape)[rows]

        mu, a0, kkc, kac = rw("mu", CT), rw("a0", 4), rw("kkc", 4), rw("kac", 4)
        rkb, w2a2, g2 = rw("rk", 4, NH), rw("w2a2", A_W), rw("g2", A_W)
        w0, gng, gnb = rw("w0", A_W), rw("gng", 4, 2, HD), rw("gnb", 4, 2, HD)
        shift, gq, gkv = rw("shift", CT, DEC_B), rw("gq", Q_LORA), rw("gkv", KV_LORA)
        R_, K_, V_ = xs[:, 0:4], xs[:, 4:8], xs[:, 8:12]

        pool_of = [view(ring, 512 * i, 4, P) for i in range(20)] + \
                  [view(work, xs_at + 512 * i, 4, P) for i in range(9)]
        names = ["Nd", "No", "Md", "G3", "G2", "G4", "N2", "M2", "N4", "M4", "XA", "XB", "WT", "UG"]
        sm = [{k: pool_of[14 * s + i] for i, k in enumerate(names)} for s in range(2)]
        for d in sm:
            d["Y"], d["M8"], d["HT"], d["H"], d["H2T"], d["TT"] = d["Md"], d["N2"], d["M2"], d["Nd"], d["N4"], d["M4"]
            d["U"] = d["UG"][:, 0:2].rearrange("p a (b v) -> p (a b) v", b=2)
            d["GV"] = d["UG"][:, 2:4].rearrange("p a (b v) -> p (a b) v", b=2)

        mo = xs_at
        ml_at = mo
        mo += ML_W
        qnT = view(work, mo, T)
        mo += T
        qlat = view(work, mo, 2, T)
        mo += 2 * T
        qlatS = view(work, mo, DEC_B, NH, DEC_T)
        mo += NH * NS
        qpeT = view(work, mo, 2, T)
        mo += 2 * T
        qpeS = view(work, mo, DEC_B, NH, DEC_T)
        mo += NH * NS
        assert mo <= WORK, mo
        oTs = view(work, 2 * NPG * P + 512, NH, DEC_B, DEC_T)
        assert 2 * NPG * P + 512 + NH * NS <= RW_W + 4 * DEC_B * HD + 4 * HD
        PGW = NPG * P
        pages_at = [xT_t, acc_t, work]
        kt = [view(t, 0, NPG, P) for t in pages_at]
        kv = [view(t, PGW, NPG, P) for t in pages_at]
        kr = [view(t, 2 * PGW, 512) for t in pages_at]
        SW = PAST + NS
        sS = view(ring, 0, 2, SW)
        pTs = view(ring, 2 * SW, 2, NPG + 1, NS)
        qpeG = view(work, ml_at, 4, DEC_B, NS)
        assert 4 * DEC_B * NS <= ML["wukT"][0]
        ro = 2 * SW + 2 * (NPG + 1) * NS
        pP = view(ring, ro, 3, 512)
        pPT = view(ring, ro + 1536, 2, 4, P)
        oT = view(ring, ro + 2560, 2, NH // 2, P)
        diag_s = view(ring, ro + 3584, NS)
        max5 = view(ring, ro + 3584 + NS, DEC_B, 5)
        sum5 = view(ring, ro + 3584 + NS + DEC_B * 5, 2, 5)
        assert ro + 3584 + NS + DEC_B * 5 + 10 <= NSLOT * SLOT
        self_scores = view(work, ml_at + ML_W, DEC_B, NS)
        assert DEC_B * NS <= T
        table = ctx.enter_context(nc.sbuf_tensor("table", [1, DEC_B * NPG], mybir.dt.int32))
        kpe_row = ctx.enter_context(nc.sbuf_tensor("kpe_row", [P, 4 * DEC_B], mybir.dt.int32))

        def mla(name, *shape):
            return view(work, ml_at + ML[name][0], *shape)

        wuqn, wuqp, wuqs = mla("wuqn", 2, NH, D_NOPE), mla("wuqp", 2, 2, P), mla("wuqs", 2, 2, P)
        wukT, wuv = mla("wukT", NH, KV_LORA), mla("wuv", NH, HD)
        def tok(tile):
            return slice(P * tile, P * tile + ROWS[tile])

        def page_ids(eng, b, pages):
            return [(i, eng.value_load(table[0:1, b * NPG + i:b * NPG + i + 1], min_val=0, max_val=A["pages"].shape[0] - 1))
                    for i in pages]

        def pages_free(eng, b):
            if b >= NPGB:
                landed(eng, job(f"Ob{b - NPGB}"), 1)
            elif pages_at[b] is work:
                eng.wait_ge(state_stored, 32)

        def load_pages(eng, b, ids, loaded):
            dst = pages_at[b % NPGB][:, 0:2 * PGW].rearrange("p (w n) -> p w n", w=2)
            for i, page in ids:
                src = A["pages"][bass.ds(page, 1), :, :].rearrange("o p n -> p (o n)")
                eng.dma_start(dst[:, :, P * i:P * i + P], src.rearrange("p (w n) -> p w n", w=2)).then_inc(loaded[b % NPGB], 16)

        def store(eng, dst, src):
            n_stores[0] += 1
            eng.dma_start(dst, src).then_inc(stored, 16)

        block = ctx.enter_context(nc.Block())

        @block.sync
        def _(sp):
            sp.dma_start(xT_t[:, :], A["xT"]).then_inc(xT_loaded, 16)
            def load(n, last_job):
                if last_job is not None:
                    take(sp, last_job)
                if BLOCKS[n][0][0] != "scratch":
                    sp.dma_start(slot(n, SLOT), A["stream"][ROW_AT[n]]).then_inc(slot_loaded[n % NSLOT], 16)

            def load_spare(layer, j):
                sp.dma_start(sparse_slot(layer, j, SLOT), A["stream"][ROW_AT[FIRST_EXPERT_BLOCK[layer] + j]])\
                    .then_inc(spare_loaded[layer][j % NSPARSE], 16)

            n = 0
            while n < len(BLOCKS):
                key = BLOCKS[n][0]
                if n == 2:
                    sp.dma_start(const[:, :], A["const"]).then_inc(const_loaded, 16)
                if n == 5:
                    sp.dma_start(x_t[:, :], A["x"]).then_inc(x_loaded, 16)
                if key[0] == "wout" and key[1:] == (1, 0):
                    sp.wait_ge(table_loaded, 32)
                    landed_all(sp, f"yT{NT - 1}")
                    for b in range(DEC_B):
                        ids = page_ids(sp, b, range(0, SP_PAGES))
                        pages_free(sp, b)
                        load_pages(sp, b, ids, page_loaded)
                if key[0] in ("w_gu", "w_down") and n - NSLOT >= FIRST_EXPERT_BLOCK[key[1]]:
                    layer = key[1]
                    rest = range(n, FIRST_EXPERT_BLOCK[layer] + 3 * N_EXP)
                    take(sp, job(f"{layer}.out", 2 * NT - 1))
                    for j in (NSLOT, NSLOT + 1):
                        load_spare(layer, j)
                    flag = is_crowded(sp, layer)
                    with sp.If(flag > 0):
                        for m in rest:
                            load(m, BLOCKS[m - NSLOT][1])
                    with sp.Else():
                        sp.wait_ge(scattered[layer], 32 * NT)
                        for j in range(NSLOT + 2, 3 * N_EXP):
                            if j >= NSPARSE:
                                take(sp, ejob(layer, (j - NSPARSE) // 3, "D1" if (j - NSPARSE) % 3 == 2 else "GU"))
                            load_spare(layer, j)
                    n = rest.stop
                    continue
                load(n, BLOCKS[n - NSLOT][1] if n >= NSLOT else None)
                n += 1

        @block.gpsimd
        def _(pool):
            def ln_params(k):
                pool.dma_start(lnp[:, :], A["ln"][k].partition_broadcast(P)).then_inc(ln_loaded, 16)

            def pool_mixture(layer):
                flag = is_crowded(pool, layer)
                with pool.If(flag > 0):
                    pool.nop()
                with pool.Else():
                    pool.wait_ge(rows_cleared, 16)
                    for tile in range(NT):
                        r = ROWS[tile]
                        for k in range(2):
                            pool.indirect_dma_start(
                                out=xrows, out_offset=bass.IndirectOffsetOnAxis(ap=rowi[0:r, 2 * tile + k:2 * tile + k + 1], axis=0),
                                in_=x[0:r, tile, :], in_offset=None).then_inc(scattered[layer], 16)
                    for e in range(N_EXP):
                        landed(pool, ejob(layer, e, "D0"), 2)
                        pool.dma_start(yrows[P * e:P * e + P, :], yS[:, e % NYS, :]).then_inc(y_stored[layer][e % NYS], 16)
                    for i in range(NYS):
                        pool.wait_ge(y_stored[layer][i], 16 * ((N_EXP - 1 - i) // NYS + 1))
                    for tile in range(NT):
                        r = ROWS[tile]
                        for k in range(2):
                            pool.indirect_dma_start(
                                out=yg[0:r, tile, k, :], out_offset=None, in_=yrows,
                                in_offset=bass.IndirectOffsetOnAxis(ap=rowi[0:r, 2 * tile + k:2 * tile + k + 1], axis=0))\
                                .then_inc(gathered[layer][tile], 16)

            pool.dma_start(even, A["even"]).then_inc(even_loaded, 16)
            pool.wait_ge(cleared, 1)
            pool.dma_start(bufT, A["buf"].rearrange("p (g b r) -> p g b r", g=HB, b=DEC_B)).then_inc(buf_loaded, 16)
            ln_params(0)
            landed_all(pool, "au")
            pool.dma_start(xrows.rearrange("(e p) d -> p e d", p=P), zero.unsqueeze(1).broadcast_to([P, N_EXP, D_MODEL]))\
                .then_inc(rows_cleared, 16)
            store(pool, outs["pool_p"].rearrange("p (g r) -> p g r", g=HB), aP[:, :, 16 + SEQ - POOL_BUF:])
            pool.wait_ge(buf_in_place, 1)
            store(pool, outs["pool_s"].rearrange("p (g b r) -> p g b r", g=HB, b=DEC_B), aS[:, :, :, DEC_T:])
            pool.wait_ge(vn_ready, NT)
            store(pool, outs["sgu"], vn[0:NS, NT - 1, :])
            landed_all(pool, "0.out")
            pool.dma_start(wr, A["wr"].rearrange("p (c e) -> p c e", c=KC)).then_inc(router_loaded, 16)
            pool.dma_start(rbias, A["rbias"]).then_inc(router_loaded, 16)
            pool.wait_ge(ln_done, NT)
            ln_params(1)
            pool_mixture(0)

            pool.dma_start(table[:, :], A["table"]).then_inc(table_loaded, 16)
            pool.dma_start(kpe_row[:, :], A["table_kpe"]).then_inc(table_loaded, 16)
            pool.wait_ge(ln_scaled, 2 * NT)
            pool.dma_start(work[:, rw_at:rw_at + RW_W], A["rwkv"]).then_inc(rwkv_loaded, 16)
            pool.dma_start(stateS, A["state"].rearrange("p (j b v) -> p j b v", j=4, b=DEC_B)).then_inc(state_loaded, 16)
            pool.wait_ge(xs_ready, CT)
            store(pool, outs["shift"].rearrange("p (c n) -> p c n", c=CT), shout)
            pool.wait_ge(mla_rows, 1)
            store(pool, outs["ckv"].rearrange("p (n c) -> p n c", n=NT), ckv)
            store(pool, outs["kpe"].rearrange("p (n c) -> p n c", n=NT), kp4[:, :, 0, :])
            landed_all(pool, f"yT{NT - 1}")
            pool.dma_start(work[:, ml_at:ml_at + ML_W], A["mla"]).then_inc(mla_loaded, 16)
            pool.dma_start(outs["state_p"].rearrange("p (j v) -> p j v", j=4), stateP).then_inc(state_stored, 16)
            pool.dma_start(outs["state_s"].rearrange("p (j b v) -> p j b v", j=4, b=DEC_B), stateS).then_inc(state_stored, 16)
            ln_params(2)
            pool.wait_ge(kpe_rows, 1)
            for b in range(DEC_B):
                ids = page_ids(pool, b, range(SP_PAGES, NPG))
                pages_free(pool, b)
                load_pages(pool, b, ids, gathered_pages)
                for i in range(4):
                    pool.indirect_dma_start(
                        out=kr[b % NPGB][:, P * i:P * i + P], out_offset=None,
                        in_=A["pages_kpe"].rearrange("g r n -> (g r) n"),
                        in_offset=bass.IndirectOffsetOnAxis(ap=kpe_row[:, 4 * b + i:4 * b + i + 1], axis=0))\
                        .then_inc(gathered_pages[b % NPGB], 16)
            pool.wait_ge(ln_done, 3 * NT)
            ln_params(3)
            pool_mixture(1)
            for tile in range(NT):
                pool.wait_ge(ln_done, (2 * LAYERS - 1) * NT + tile + 1)
                store(pool, outs["x"][:, D_MODEL * tile:D_MODEL * tile + D_MODEL], x[:, tile, :])
            pool.wait_ge(stored, 16 * n_stores[0])
            pool.wait_ge(state_stored, 32)

        @block.tensor
        def _(pe):
            def transpose_x(name, norm, then=None):
                for tile in range(NT):
                    if then and tile > 1:
                        then(tile - 2)
                    r = ROWS[tile]
                    if norm:
                        pe.wait_ge(ln_done, NT * (norm - 1) + tile + 1)
                    for g in range(2):
                        n = job(name, 2 * tile + g)
                        claim(pe, n)
                        for k in range(4):
                            i = pe.transpose(bank(n, 4, P)[:, k, 0:r], x[0:r, tile, P * (4 * g + k):P * (4 * g + k + 1)],
                                             ident[0:r, 0:r])
                        done(i, n)

            def out_projection(layer, name):
                for half in range(2):
                    w = [weights(pe, ("wout", layer, 2 * half + q)) for q in range(2)]
                    for tile in range(NT):
                        n = job(name, NT * half + tile)
                        claim(pe, n)
                        for q in range(2):
                            for k in range(KC):
                                i = pe.matmul(bank(n)[0:ROWS[tile], 256 * q:256 * q + 256], cat[:, k, tok(tile)],
                                              slot(w[q], KC, 256)[:, k, :], start=(k == 0), stop=(k == KC - 1))
                        done(i, n)

            def mixture(layer):
                L = f"{layer}."

                def router_scores(tile):
                    n = job(L + "router")
                    if tile == 0:
                        pe.wait_ge(router_loaded, 32)
                        claim(pe, n)
                    landed(pe, job(L + "mT", 2 * tile), 2)
                    for k in range(KC):
                        i = pe.matmul(bank(n, NT, N_EXP)[0:ROWS[tile], tile, :], xT[:, k, tok(tile)], wr[:, k, :],
                                      start=(k == 0), stop=(k == KC - 1))
                    if tile == NT - 1:
                        done(i, n)

                transpose_x(L + "mT", 2 * layer + 1, router_scores)
                router_scores(NT - 2)
                router_scores(NT - 1)
                n = job(L + "pos")
                pe.wait_ge(sel_ready, layer + 1)
                claim(pe, n)
                pos = bank(n, NT + 1, N_EXP)
                for tile in range(NT + 1):
                    m = P if tile == NT else ROWS[tile]
                    for q in range(min(tile, NT - 1) + 1):
                        r = ROWS[q]
                        tri = c("before", r)[:, 0:m] if q == tile else c("ones", r)[:, 0:m]
                        i = pe.matmul(pos[0:m, tile, :], tri, both[0:r, q, :], start=(q == 0),
                                      stop=(q == min(tile, NT - 1)))
                done(i, n)
                flag = is_crowded(pe, layer)
                with pe.If(flag > 0):
                    every_expert(layer)
                with pe.Else():
                    own_tokens(layer)

            def own_tokens(layer):
                def turn_rows(e):
                    pe.wait_ge(xg_loaded[layer][e % NXG], 16 * (e // NXG + 1))
                    for g in range(2):
                        n = ejob(layer, e, f"T{g}")
                        claim(pe, n)
                        for k in range(4):
                            i = pe.transpose(bank(n, 4, P)[:, k, :], xg[:, e % NXG, P * (4 * g + k):P * (4 * g + k + 1)], ident)
                        done(i, n)

                def hidden(e):
                    for q in range(2):
                        sparse_weights(pe, layer, 3 * e + q)
                    landed(pe, ejob(layer, e, "T0"), 2)
                    n = ejob(layer, e, "GU")
                    claim(pe, n)
                    for k in range(KC):
                        i = pe.matmul(bank(n), xgT[:, e % 2, k, :],
                                      sparse_slot(layer, 3 * e + k // 4, 4, 512)[:, k % 4, :],
                                      start=(k == 0), stop=(k == KC - 1))
                    done(i, n)

                def turn_hidden(e):
                    landed(pe, ejob(layer, e, "GU"), 1)
                    n = ejob(layer, e, "HT")
                    claim(pe, n)
                    for k in range(2):
                        i = pe.transpose(bank(n, 4, P)[:, k, :], hS[:, e % 2, P * k:P * k + P], ident)
                    done(i, n)

                def output(e):
                    sparse_weights(pe, layer, 3 * e + 2)
                    landed(pe, ejob(layer, e, "HT"), 1)
                    for half in range(2):
                        n = ejob(layer, e, f"D{half}")
                        claim(pe, n)
                        for k in range(2):
                            i = pe.matmul(bank(n), hTS[:, e % 2, k, :],
                                          sparse_slot(layer, 3 * e + 2, 2, D_MODEL)[:, k, 512 * half:512 * half + 512],
                                          start=(k == 0), stop=(k == 1))
                        done(i, n)

                turn_rows(0)
                for e in range(N_EXP + 1):
                    if e + 1 < N_EXP:
                        turn_rows(e + 1)
                    if e > 0:
                        turn_hidden(e - 1)
                    if e < N_EXP:
                        hidden(e)
                    if e > 0:
                        output(e - 1)

            def every_expert(layer):
                L = f"{layer}."
                for j in (NSLOT, NSLOT + 1):
                    pe.wait_ge(spare_loaded[layer][j], 16)
                for e in range(N_EXP):
                    w = [weights(pe, ("w_gu", layer, e, q)) for q in range(2)]
                    for m in range(2):
                        for s, (a, nn) in enumerate(SPLITS):
                            for u in range(2):
                                n = job(f"{L}e{e}", 4 * m + 2 * s + u)
                                claim(pe, n)
                                for k in range(KC):
                                    at = D_EXP * u + P * m
                                    i = pe.matmul(bank(n)[:, 0:nn], slot(w[k // 4], 4, 512)[:, k % 4, at:at + P],
                                                  xT[:, k, a:a + nn], start=(k == 0), stop=(k == KC - 1))
                                done(i, n)
                    w = weights(pe, ("w_down", layer, e))
                    landed(pe, job(f"{L}e{e}"), 8)
                    for half in range(2):
                        for tile in range(NT):
                            n = job(f"{L}e{e}", 8 + NT * half + tile)
                            claim(pe, n)
                            for k in range(2):
                                i = pe.matmul(bank(n)[0:ROWS[tile], :], hT[:, e % 2, k, tok(tile)],
                                              slot(w, 2, D_MODEL)[:, k, 512 * half:512 * half + 512],
                                              start=(k == 0), stop=(k == 1))
                            done(i, n)

            pe.wait_ge(xT_loaded, 16)
            for m in range(8):
                w = weights(pe, ("ein", m // 2))
                for s, (a, nn) in enumerate(SPLITS):
                    n = job("au", 2 * m + s)
                    claim(pe, n)
                    for k in range(KC):
                        i = pe.matmul(bank(n)[:, 0:nn], slot(w, KC, 256)[:, k, P * (m % 2):P * (m % 2) + P],
                                      xT[:, k, a:a + nn], start=(k == 0), stop=(k == KC - 1))
                    done(i, n)
            w = [weights(pe, ("ein", 4 + q)) for q in range(2)]
            for tile in range(NT):
                n = job("v", tile)
                claim(pe, n)
                for q in range(2):
                    for k in range(KC):
                        i = pe.matmul(bank(n)[0:ROWS[tile], 256 * q:256 * q + 256], xT[:, k, tok(tile)],
                                      slot(w[q], KC, 256)[:, k, :], start=(k == 0), stop=(k == KC - 1))
                done(i, n)
            pe.wait_ge(even_loaded, 16)
            for g in range(HB):
                pe.wait_ge(pooled_ready, 2 * g + 2)
                for s, (a, nn) in enumerate(SPLITS):
                    n = job("pool", 2 * g + s)
                    claim(pe, n)
                    done(pe.matmul(bank(n)[:, 0:nn], poolw[:, g, :], pooled[:, g, a:a + nn], start=True, stop=True), n)
            pe.wait_ge(mask_applied, 1)
            for tile in range(NT):
                r = ROWS[tile]
                pe.wait_ge(vn_ready, tile + 1)
                n = job("mix", tile)
                claim(pe, n)
                for h in range(HB):
                    w = WT[:, h, :] if r == P else WTs[0:r, h, :]
                    i = pe.matmul(bank(n, HB, P)[:, h, 0:r], vn[0:r, tile, P * h:P * h + P], w, start=True, stop=True)
                done(i, n)
            landed_all(pe, "pool")
            landed_all(pe, "mix")
            out_projection(0, "0.out")
            mixture(0)

            def odd():
                transpose_x("xT", 2)
                landed_all(pe, "xT")
                for m in range(CT):
                    w = weights(pe, ("oin", m // 2))
                    for s, (a, nn) in enumerate(SPLITS):
                        n = job("c", 2 * m + s)
                        claim(pe, n)
                        for k in range(KC):
                            i = pe.matmul(bank(n)[:, 0:nn], slot(w, KC, 256)[:, k, P * (m % 2):P * (m % 2) + P],
                                          xT[:, k, a:a + nn], start=(k == 0), stop=(k == KC - 1))
                        done(i, n)
                w = [weights(pe, ("oin", 7 + q)) for q in range(2)]
                for tile in range(NT):
                    n = job("dtok", tile)
                    claim(pe, n)
                    for q in range(2):
                        for k in range(KC):
                            b = min(256 * q + 256, D_COLS)
                            i = pe.matmul(bank(n)[0:ROWS[tile], 256 * q:b], xT[:, k, tok(tile)],
                                          slot(w[q], KC, 256)[:, k, 0:b - 256 * q], start=(k == 0), stop=(k == KC - 1))
                    done(i, n)
                pe.wait_ge(gate_in, 1)
                for tile in range(NT):
                    n = job("decay", tile)
                    claim(pe, n)
                    done(pe.matmul(bank(n)[0:ROWS[tile], :], xs[0:64, 12, tok(tile)], w2a2[0:64, :],
                                   start=True, stop=True), n)
                for m in range(4):
                    for s, (a, nn) in enumerate(SPLITS):
                        n = job("iclr", 2 * m + s)
                        claim(pe, n)
                        done(pe.matmul(bank(n)[:, 0:nn], w2a2[64:128, P * m:P * m + P], xs[64:128, 12, a:a + nn],
                                       start=True, stop=True), n)
                pe.wait_ge(sq_ready, 1)
                for m in range(4):
                    for s, (a, nn) in enumerate(SPLITS):
                        n = job("norm", 2 * m + s)
                        claim(pe, n)
                        done(pe.matmul(bank(n)[:, 0:nn], c("headof"), rho[:, m, a:a + nn], start=True, stop=True), n)
                pe.wait_ge(mla_rows, 1)
                for tile in range(NT):
                    r = ROWS[tile]
                    n = job("dT", tile)
                    claim(pe, n)
                    srcs = [pd[0:r, tile, 0:P], pd[0:r, tile, P:2 * P], ckv[0:r, tile, :],
                            kp4[0:r, tile].rearrange("p a b -> p (a b)")]
                    for k, src in enumerate(srcs):
                        i = pe.transpose(bank(n, 4, P)[:, k, 0:r], src, ident[0:r, 0:r])
                    done(i, n)
                pe.wait_ge(bonus_in, 1)
                n = job("bonus")
                claim(pe, n)
                for tile in range(NT):
                    for j in range(4):
                        i = pe.matmul(bank(n, NT, NH)[0:ROWS[tile], tile, :], K_[:, j, tok(tile)], rkb[:, j, :],
                                      start=(j == 0), stop=(j == 3))
                done(i, n)
                pe.wait_ge(ld_ready, NT)
                for tile in range(NT):
                    r = ROWS[tile]
                    tri = c("cum") if r == P else c("scum", r)
                    for q in range(2):
                        n = job("cum", 2 * tile + q)
                        claim(pe, n)
                        for k in range(2):
                            m = 2 * q + k
                            i = pe.matmul(bank(n, 2, 256)[:, k, 0:2 * r], ld[0:r, tile, P * m:P * m + P], tri,
                                          start=True, stop=True)
                        done(i, n)
                pe.wait_ge(scaled_ready, 2 * NT)
                for tile in range(NT):
                    recurrence(tile)
                latent_attention()

            def recurrence(tile):
                r = ROWS[tile]
                prompt = tile < NT - 1
                for k, src in enumerate((alpha, V_, beta, kappa)):
                    n = job(f"tok{tile}", k)
                    claim(pe, n)
                    for j in range(4):
                        i = pe.transpose(bank(n, 4, P)[0:r, j, :], src[:, j, tok(tile)], ident)
                    done(i, n)
                tk = lambda k, j, s: tokm[0:r, k, j, s, :]
                product = {"G3": (beta, rho), "G2": (kappa, alpha), "G4": (kappa, rho), "MT": (beta, alpha),
                           "M": (alpha, beta)}
                square = {"N2": ("Md", "Nd"), "M2": ("Nd", "Md"), "N4": ("M2", "N2"), "M4": ("N2", "M2"),
                          "M8": ("N4", "M4"), "X1": ("M2", "XA"), "X2": ("M4", "XB"), "X3": ("M8", "XA"),
                          "HT": ("No", "Y"), "H": ("Y", "No"), "H2T": ("H", "HT"), "Z": ("H2T", "XB"),
                          "TT": ("HT", "XA")}
                reads = {"N2": ("MT", "M"), "M2": ("MT", "M"), "N4": ("N2", "M2"), "M4": ("N2", "M2"),
                         "M8": ("N4", "M4"), "X1": ("M2",), "X2": ("M4", "X1"), "X3": ("M8", "X2"), "Y": ("X3",),
                         "HT": ("Y",), "H": ("Y",), "H2T": ("H", "HT"), "Z": ("H2T",), "TT": ("Z",),
                         "G2V": ("G2",), "U": ("G2V", "TT" if prompt else "X2"), "WT": ("TT" if prompt else "X2",)}
                for step_name in (STEPS if prompt else STEPS_S):
                    for s in range(2):
                        d = sm[s]
                        tt = d["TT"] if prompt else d["XA"]
                        p0 = slice(HD * s, HD * s + HD)
                        n = unit_job(tile, step_name, s)
                        for name in reads.get(step_name, ()):
                            landed(pe, unit_job(tile, name, s), 1)
                        if step_name == "G2V" and s == 0:
                            landed_all(pe, f"tok{tile}")
                        if step_name == "X1":
                            pe.wait_ge(x0_ready, 2 * tile + s + 1)
                        claim(pe, n)
                        for j in range(4):
                            if step_name in product:
                                a, b = product[step_name]
                                i = pe.matmul(bank(n, 4, P)[0:r, j, 0:r], a[p0, j, tok(tile)], b[p0, j, tok(tile)],
                                              start=True, stop=True)
                            elif step_name in square:
                                a, b = square[step_name]
                                i = pe.matmul(bank(n, 4, P)[0:r, j, 0:r], d[a][0:r, j, 0:r], d[b][0:r, j, 0:r],
                                              start=True, stop=True)
                            elif step_name == "Y":
                                i = pe.transpose(bank(n, 4, P)[0:r, j, 0:r], d["XB"][0:r, j, 0:r], ident[0:r, 0:r])
                            elif step_name == "G2V":
                                i = pe.matmul(bank(n)[0:r, HD * j:HD * j + HD], d["G2"][0:r, j, 0:r], tk(1, j, s),
                                              start=True, stop=True)
                            elif step_name == "U":
                                i = pe.matmul(bank(n)[0:r, HD * j:HD * j + HD], tt[0:r, j, 0:r], d["GV"][0:r, j, :],
                                              start=True, stop=True)
                            else:
                                i = pe.matmul(bank(n, 4, P)[p0, j, 0:r], tk(0, j, s), tt[0:r, j, 0:r],
                                              start=True, stop=True)
                        done(i, n)
                for s in range(2):
                    landed(pe, unit_job(tile, "WT", s), 1)
                if prompt:
                    for ch in range(2):
                        rc = slice(CH * ch, CH * ch + CH)
                        if tile == 0 and ch == 0:
                            pe.wait_ge(state_reset, 1)
                        else:
                            prev = job(f"chain{tile - (ch == 0)}", 3 * (1 - ch) + 2)
                            landed(pe, prev, 1)
                        for s in range(2):
                            p0 = slice(HD * s, HD * s + HD)
                            n = job(f"chain{tile}", 3 * ch + s)
                            claim(pe, n)
                            for j in range(4):
                                pe.matmul(bank(n)[rc, HD * j:HD * j + HD], sm[s]["WT"][p0, j, rc], stateP[p0, j, :],
                                          start=True, stop=True)
                                i = pe.matmul(bank(n)[rc, 256 + HD * j:256 + HD * j + HD],
                                              rho[p0, j, P * tile + CH * ch:P * tile + CH * ch + CH],
                                              stateP[p0, j, :], start=True, stop=True)
                            done(i, n)
                        n = job(f"chain{tile}", 3 * ch + 2)
                        landed(pe, n - 2, 2)
                        claim(pe, n)
                        for j in range(4):
                            for s in range(2):
                                p0 = slice(HD * s, HD * s + HD)
                                pe.matmul(bank(n)[p0, HD * j:HD * j + HD], tokm[rc, 2, j, s, :], p_sb[rc, j, s, :],
                                          start=True, stop=False)
                                i = pe.matmul(bank(n)[p0, HD * j:HD * j + HD], tokm[rc, 3, j, s, :],
                                              tokm[rc, 1, j, s, :], start=False, stop=True)
                        done(i, n)
                else:
                    pe.wait_ge(state_loaded, 16)
                    def with_states(h):
                        j, s = h // 2, h % 2
                        p0 = slice(HD * s, HD * s + HD)
                        for k, w in enumerate((sm[s]["WT"][p0, j, 0:r], rho[p0, j, tok(tile)])):
                            n = state_job(h, k)
                            claim(pe, n)
                            done(pe.matmul(bank(n)[0:r, :], w, stateS[p0, j].rearrange("p b v -> p (b v)"),
                                           start=True, stop=True), n)

                    with_states(0)
                    for h in range(NH):
                        j, s = h // 2, h % 2
                        p0 = slice(HD * s, HD * s + HD)
                        if h + 1 < NH:
                            with_states(h + 1)
                        n = state_job(h, 2)
                        pe.wait_ge(psel_ready, h + 1)
                        claim(pe, n)
                        pe.matmul(bank(n)[p0, :], tokm[0:r, 2, j, s, :], sm[s]["No"][0:r].rearrange("p a b -> p (a b)"),
                                  start=True, stop=False)
                        done(pe.matmul(bank(n)[p0, :], tokm[0:r, 3, j, s, :],
                                       sm[s]["Md"][0:r].rearrange("p a b -> p (a b)"), start=False, stop=True), n)
                n = job(f"y{tile}", 0)
                claim(pe, n)
                for j in range(4):
                    for s in range(2):
                        dst = bank(n, 4, 2, HD)[0:r, j, s, :]
                        pe.matmul(dst, sm[s]["G3"][0:r, j, 0:r], p_sb[0:r, j, s, :], start=True, stop=False)
                        i = pe.matmul(dst, sm[s]["G4"][0:r, j, 0:r], tk(1, j, s), start=False, stop=True)
                done(i, n)
                n = job(f"y{tile}", 1)
                claim(pe, n)
                done(pe.matmul(bank(n)[0:r, :], xs[:, 13, tok(tile)], g2, start=True, stop=True), n)
                n = job(f"yT{tile}")
                landed(pe, job(f"y{tile}", 1), 1)
                claim(pe, n)
                for j in range(4):
                    i = pe.transpose(bank(n, 4, P)[:, j, 0:r], y_sb[0:r, j].rearrange("p s v -> p (s v)"), ident[0:r, 0:r])
                done(i, n)

            def latent_attention():
                pe.wait_ge(mla_loaded, 16)
                for g in range(2):
                    for s, (a, nn) in enumerate(SPLITS):
                        for k, w in enumerate((wuqp, wuqs)):
                            n = job("qpe", 4 * g + 2 * s + k)
                            claim(pe, n)
                            for kk in range(2):
                                i = pe.matmul(bank(n)[:, 0:nn], w[:, kk, g, :], cqT[:, kk, a:a + nn],
                                              start=(kk == 0), stop=(kk == 1))
                            done(i, n)
                pe.wait_ge(qpe_ready, 1)

                def latent_query(h, part):
                    for s, (a, nn) in enumerate(SPLITS):
                        n = job(f"q{h}{part}", s)
                        claim(pe, n)
                        if part == "a":
                            for kk in range(2):
                                i = pe.matmul(bank(n)[0:D_NOPE, 0:nn], wuqn[:, kk, h, :], cqT[:, kk, a:a + nn],
                                              start=(kk == 0), stop=(kk == 1))
                        else:
                            landed(pe, job(f"q{h}a", s), 1)
                            i = pe.matmul(bank(n)[:, 0:nn], wukT[0:D_NOPE, h, :], qnT[0:D_NOPE, a:a + nn],
                                          start=True, stop=True)
                        done(i, n)

                def scores(u):
                    h, t = u // 4, u % 4
                    if t == 0:
                        landed(pe, job(f"q{h}b"), 2)
                    n = job(f"S{u}")
                    claim(pe, n)
                    keys = P * (t + 1)
                    q = slice(32 * (h % 4), 32 * (h % 4) + 32)
                    pe.matmul(bank(n)[:, 0:keys], qlat[:, h % 2, P * t:P * t + P], ckvT[:, 0:keys], start=True, stop=False)
                    done(pe.matmul(bank(n)[:, 0:keys], qpeT[q, h // 4, P * t:P * t + P], kpeT[q, 0:keys],
                                   start=False, stop=True, tile_position=(32 * (h % 4), 0)), n)

                def turn(u):
                    n = job(f"PT{u}")
                    pe.wait_ge(snorm, u + 1)
                    claim(pe, n)
                    for k in range(u % 4 + 1):
                        i = pe.transpose(bank(n, 4, P)[:, k, :], pP[:, u % 3, P * k:P * k + P], ident)
                    done(i, n)

                def values(u):
                    t = u % 4
                    landed(pe, job(f"PT{u}"), 1)
                    n = job(f"O{u}")
                    claim(pe, n)
                    for k in range(t + 1):
                        i = pe.matmul(bank(n)[:, 0:P], ckv[:, k, :], pPT[:, u % 2, k, :], start=(k == 0), stop=(k == t))
                    done(i, n)

                def head_out(h):
                    landed(pe, job(f"O{4 * h + 3}"), 1)
                    n = job(f"yd{h}")
                    claim(pe, n)
                    p0 = slice(HD * (h % 2), HD * (h % 2) + HD)
                    done(pe.matmul(bank(n)[p0, :], wuv[:, h, :], oT[:, h % 2].rearrange("p a b -> p (a b)"),
                                   start=True, stop=True), n)

                latent_query(0, "a")
                latent_query(0, "b")
                for u in range(N_ATT + LAG + 2):
                    if u < N_ATT:
                        scores(u)
                        if u % 4 in (1, 2) and u + 4 < N_ATT:
                            latent_query(u // 4 + 1, "ab"[u % 4 - 1])
                    if 0 <= u - LAG < N_ATT:
                        turn(u - LAG)
                    if 0 <= u - LAG - 1 < N_ATT:
                        values(u - LAG - 1)
                    if u - LAG - 2 >= 0 and (u - LAG - 2) % 4 == 3:
                        head_out((u - LAG - 2) // 4)

                def batch_scores(b, groups):
                    pe.wait_ge(page_loaded[b % NPGB], 16 * SP_PAGES * (b // NPGB + 1))
                    pe.wait_ge(gathered_pages[b % NPGB], 16 * (4 + NPG - SP_PAGES) * (b // NPGB + 1))
                    for g in groups:
                        n = batch_job(b, g)
                        claim(pe, n)
                        pe.matmul(bank(n)[0:NS, :], qlatS[:, b].rearrange("p h t -> p (h t)"),
                                  kt[b % NPGB][:, 4 * g:4 * g + 4, :], start=True, stop=False)
                        done(pe.matmul(bank(n)[0:NS, :], qpeG[:, g, b, :], kr[b % NPGB][:, :], start=False, stop=True), n)

                def batch_turn(b):
                    pe.wait_ge(snorm_s, b + 1)
                    for g in range(3):
                        n = job(f"PTb{b}", g)
                        claim(pe, n)
                        for k in range(8 if g < 2 else 1):
                            at = P * (8 * g + k)
                            width = P if g < 2 else NS
                            i = pe.matmul(bank(n, 8, NS)[0:width, k, :], sS[0:NS, b % 2, at:at + width],
                                          diag_s[0:NS, :], start=True, stop=True)
                        done(i, n)

                def batch_values(b):
                    landed_all(pe, f"PTb{b}")
                    n = job(f"Ob{b}")
                    claim(pe, n)
                    for k in range(NPG):
                        pe.matmul(bank(n)[:, 0:NS], kv[b % NPGB][:, k, :], pTs[:, b % 2, k, :], start=(k == 0), stop=False)
                    done(pe.matmul(bank(n)[:, 0:NS], ckv[0:NS, NT - 1, :], pTs[0:NS, b % 2, NPG, :],
                                   start=False, stop=True), n)

                pe.wait_ge(groups_ready, 1)
                n = job("own")
                claim(pe, n)
                for b in range(DEC_B):
                    dst = bank(n, DEC_B, NS)[0:NS, b, :]
                    pe.matmul(dst, qlatS[:, b].rearrange("p h t -> p (h t)"), ckvT[:, SEQ:T], start=True, stop=False)
                    i = pe.matmul(dst, qpeG[:, 0, b, :], kpeT[:, SEQ:T], start=False, stop=True)
                done(i, n)
                for b in range(DEC_B + 1):
                    if b < DEC_B:
                        batch_scores(b, range(3))
                    if b > 0:
                        batch_turn(b - 1)
                    if b < DEC_B:
                        batch_scores(b, (3,))
                    if b > 0:
                        batch_values(b - 1)
                for b in range(DEC_B):
                    landed(pe, job(f"Ob{b}"), 1)
                n = job("ydS")
                claim(pe, n)
                for h in range(NH):
                    p0 = slice(HD * (h % 2), HD * (h % 2) + HD)
                    i = pe.matmul(bank(n)[p0, NS * (h // 2):NS * (h // 2) + NS], wuv[:, h, :],
                                  oTs[:, h].rearrange("p b t -> p (b t)"), start=True, stop=True)
                done(i, n)
                landed(pe, n, 1)

            if LAYERS > 1:
                odd()
                out_projection(1, "1.out")
                mixture(1)

        @block.scalar
        def _(act):
            step = stepper(act, act_step)

            def copy_xT(name):
                for tile in range(NT):
                    for g in range(2):
                        n = job(name, 2 * tile + g)
                        take(act, n)
                        give(act.copy(xT[:, 4 * g:4 * g + 4, tok(tile)], bank(n, 4, P)[:, :, 0:ROWS[tile]]), n)

            def norm(k):
                act.wait_ge(ln_var, k + 1)
                act.activation(rstd, rstd, ACT.Sqrt).then_inc(ln_std, 1)
                act.wait_ge(ln_affine, k + 1)
                for tile in range(NT):
                    r = ROWS[tile]
                    act.activation(x[0:r, tile, :], acc[0:r, tile, :], ACT.Identity, bias=nmr[0:r, tile:tile + 1],
                                   scale=rstd[0:r, tile:tile + 1]).then_inc(ln_scaled, 1)

            def mixture(layer):
                L = f"{layer}."
                copy_xT(L + "mT")
                n = job(L + "router")
                take(act, n)
                act.activation(score[:, 0:4, :], bank(n, NT, N_EXP)[:, 0:4, :], ACT.Sigmoid).then_inc(act_step, 1)
                give(act.activation(score[0:NS, 4, :], bank(n, NT, N_EXP)[0:NS, 4, :], ACT.Sigmoid), n)
                flag = is_crowded(act, layer)
                with act.If(flag > 0):
                    for e in range(N_EXP):
                        for m in range(2):
                            for s, (a, nn) in enumerate(SPLITS):
                                n = job(f"{L}e{e}", 4 * m + 2 * s)
                                take(act, n)
                                give(act.activation(hg[:, e % 2, m, a:a + nn], bank(n)[:, 0:nn], ACT.Silu), n)
                with act.Else():
                    def load_rows(e):
                        act.dma_start(xg[:, e % NXG, :], xrows[P * e:P * e + P, :]).then_inc(xg_loaded[layer][e % NXG], 16)

                    act.wait_ge(scattered[layer], 32 * NT)
                    for e in range(NXG):
                        load_rows(e)
                    for e in range(-1, N_EXP + 1):
                        if e + 1 < N_EXP:
                            n = ejob(layer, e + 1, "T0")
                            take(act, n)
                            give(act.copy(xgT[:, (e + 1) % 2, 0:4, :], bank(n, 4, P)), n)
                        if e > 0:
                            n = ejob(layer, e - 1, "HT")
                            take(act, n)
                            give(act.copy(hTS[:, (e - 1) % 2, :, :], bank(n, 2, P)), n)
                        if 0 <= e < N_EXP:
                            n = ejob(layer, e, "GU")
                            take(act, n)
                            if e > 0:
                                landed(act, ejob(layer, e - 1, "GU"), 1)
                            act.activation(hgS, bank(n)[:, 0:D_EXP], ACT.Silu).then_inc(silu_done[layer], 1)
                            if e + NXG < N_EXP:
                                take(act, ejob(layer, e, "T1"))
                                load_rows(e + NXG)
                        if e > 0:
                            n = ejob(layer, e - 1, "D0")
                            if e - 1 >= NYS:
                                act.wait_ge(y_stored[layer][(e - 1) % NYS], 16 * ((e - 1) // NYS))
                            take(act, n)
                            give(act.copy(yS[:, (e - 1) % NYS, 0:512], bank(n)), n)
                norm(2 * layer + 1)

            for m in range(4, 8):
                for s, (a, nn) in enumerate(SPLITS):
                    n = job("au", 2 * m + s)
                    take(act, n)
                    give(act.activation(uT[:, m - 4, a:a + nn], bank(n)[:, 0:nn], ACT.Gelu), n)
            for tile in range(NT):
                n = job("v", tile)
                take(act, n)
                give(act.activation(vn[0:ROWS[tile], tile, :], bank(n)[0:ROWS[tile], :], ACT.Gelu), n)
            act.wait_ge(even_loaded, 16)
            for g in range(HB):
                for s, (a, nn) in enumerate(SPLITS):
                    n = job("pool", 2 * g + s)
                    take(act, n)
                    give(act.activation(cat[:, g, a:a + nn], bank(n)[:, 0:nn], ACT.Copy, scale=pscale[:, g:g + 1]), n)
            act.wait_ge(vn_var, 1)
            act.activation(vrstd, vrstd, ACT.Sqrt).then_inc(vn_std, 1)
            norm(0)
            mixture(0)

            def odd():
                copy_xT("xT")
                for m in range(CT):
                    for s in range(2):
                        n = job("c", 2 * m + s)
                        take(act, n)
                        act.wait_ge(pc_begun, max(m + 1, 2))
                        if s == 0:
                            give(act.copy(pc[:, m % 2, 1:1 + SEQ], bank(n)), n)
                        else:
                            give(act.copy(pc[:, m % 2, 1 + SEQ:].rearrange("p (b t) -> p b t", b=DEC_B)[:, :, 1:],
                                          bank(n, DEC_B, DEC_T)), n)
                act.wait_ge(xs_ready, CT)
                act.activation(xs[0:64, 12, :], xs[0:64, 12, :], ACT.Tanh).then_inc(act_step, 1)
                act.activation(xs[:, 13, :], xs[:, 13, :], ACT.Sigmoid).then_inc(gate_in, 1)
                act.wait_ge(rms_sum, 1)
                act.activation(srs, srs, ACT.Sqrt).then_inc(rms_std, 1)
                for tile in range(NT):
                    r = ROWS[tile]
                    landed(act, job("decay", tile), 1)
                    act.activation(ld[0:r, tile, :], ld[0:r, tile, :], ACT.Sigmoid).then_inc(ld_ready, 1)
                for m in range(4):
                    for s, (a, nn) in enumerate(SPLITS):
                        n = job("iclr", 2 * m + s)
                        take(act, n)
                        give(act.activation(beta[:, m, a:a + nn], bank(n)[:, 0:nn], ACT.Sigmoid, bias=a0[:, m:m + 1]), n)
                act.wait_ge(kk_sum, 1)
                act.activation(rho, rho, ACT.Sqrt).then_inc(kk_std, 1)
                for tile in range(NT):
                    r = ROWS[tile]
                    n = job("dT", tile)
                    take(act, n)
                    act.copy(cqT[:, :, tok(tile)], bank(n, 4, P)[:, 0:2, 0:r])
                    act.copy(ckvT[:, tok(tile)], bank(n, 4, P)[:, 2, 0:r])
                    give(act.copy(kpeT[:, tok(tile)], bank(n, 4, P)[:, 3, 0:r]), n)
                for tile in range(NT):
                    r = ROWS[tile]
                    for q in range(2):
                        i = 2 * tile + q
                        n = job("cum", i)
                        take(act, n)
                        if i == 0:
                            landed_all(act, "dT")
                        if i >= 2:
                            act.wait_ge(scaled_ready, i - 1)
                        e = expo[:, i % 2]
                        incl, excl = bank(n, 2, 256)[:, :, 0:r], bank(n, 2, 256)[:, :, r:2 * r]
                        act.activation(e[:, 0, :, 0:r], incl, ACT.Exp, scale=-DECAY)
                        act.activation(e[:, 1, :, 0:r], excl, ACT.Exp, scale=-DECAY)
                        give(act.activation(e[:, 2, :, 0:r], incl, ACT.Exp, scale=DECAY), n)
                for tile in range(NT):
                    recurrence(tile)
                latent_attention()

            def recurrence(tile):
                r = ROWS[tile]
                prompt = tile < NT - 1
                if tile == 0:
                    act.wait_ge(scaled_ready, 2 * NT)
                else:
                    landed(act, job(f"y{tile - 1}", 1), 1)
                for k in (0, 2):
                    n = job(f"tok{tile}", k)
                    take(act, n)
                    give(act.activation(tokm[0:r, k].rearrange("p a s v -> p a (s v)"), bank(n, 4, P)[0:r, :, :], ACT.Copy,
                                        scale=(-1.0 if k == 2 else 1.0)), n)
                for step_name in (STEPS if prompt else STEPS_S):
                    for s in range(2):
                        n = unit_job(tile, step_name, s)
                        d = sm[s]
                        if step_name in ("N2", "M2", "N4", "M4", "M8", "Y", "HT", "H", "H2T"):
                            take(act, n)
                            give(act.copy(d[step_name][0:r, :, 0:r], bank(n, 4, P)[0:r, :, 0:r]), n)
                        elif step_name == "G2V":
                            take(act, n)
                            give(act.copy(d["GV"][0:r], bank(n, 4, HD)[0:r]), n)
                        elif step_name == "U":
                            take(act, n)
                            give(act.copy(d["U"][0:r], bank(n, 4, HD)[0:r]), n)
                        elif step_name == "WT":
                            take(act, n)
                            p0 = slice(HD * s, HD * s + HD)
                            give(act.copy(d["WT"][p0, :, 0:r], bank(n, 4, P)[p0, :, 0:r]), n)
                act.wait_ge(gn_var, tile + 1)
                act.activation(grs[0:r], grs[0:r], ACT.Sqrt).then_inc(gn_std, 1)
                n = job(f"yT{tile}")
                take(act, n)
                give(act.copy(cat[:, 0:4, tok(tile)], bank(n, 4, P)[:, :, 0:r]), n)

            def latent_attention():
                def latent_query(h, part):
                    for s, (a, nn) in enumerate(SPLITS):
                        n = job(f"q{h}{part}", s)
                        take(act, n)
                        if part == "a":
                            give(act.copy(qnT[0:D_NOPE, a:a + nn], bank(n)[0:D_NOPE, 0:nn]), n)
                        elif s == 0:
                            give(act.copy(qlat[:, h % 2, 0:nn], bank(n)[:, 0:nn]), n)
                        else:
                            give(act.copy(qlatS[:, :, h, :], bank(n, DEC_B, DEC_T)), n)

                def weigh(u):
                    act.wait_ge(smax, u + 1)
                    keys = P * (u % 4 + 1)
                    n = job(f"S{u}")
                    if u >= 3:
                        take(act, job(f"PT{u - 3}"))
                    give(act.activation(pP[:, u % 3, 0:keys], bank(n)[:, 0:keys], ACT.Exp, scale=MLA_SCALE,
                                        bias=rmax[:, u % 2:u % 2 + 1], accum_out=rsum[:, u % 2:u % 2 + 1]), n)

                latent_query(0, "a")
                latent_query(0, "b")
                for u in range(N_ATT + LAG + 2):
                    if u < N_ATT:
                        if u % 4 in (1, 2) and u + 4 < N_ATT:
                            latent_query(u // 4 + 1, "ab"[u % 4 - 1])
                        weigh(u)
                    if 0 <= u - LAG < N_ATT:
                        v = u - LAG
                        n = job(f"PT{v}")
                        if v >= 2:
                            take(act, job(f"O{v - 2}"))
                        take(act, n)
                        give(act.copy(pPT[:, v % 2, 0:v % 4 + 1, :], bank(n, 4, P)[:, 0:v % 4 + 1, :]), n)
                    if 0 <= u - LAG - 1 < N_ATT:
                        v = u - LAG - 1
                        n = job(f"O{v}")
                        if v >= 8:
                            take(act, job(f"yd{v // 4 - 2}"))
                        take(act, n)
                        give(act.copy(oT[:, v // 4 % 2, v % 4, :], bank(n)[:, 0:P]), n)

                for b in range(DEC_B + 1):
                    for g in range(3 if b > 0 else 0):
                        n = job(f"PTb{b - 1}", g)
                        take(act, n)
                        if g < 2:
                            give(act.copy(pTs[:, (b - 1) % 2, 8 * g:8 * g + 8, :], bank(n, 8, NS)), n)
                        else:
                            give(act.copy(pTs[0:NS, (b - 1) % 2, NPG, :], bank(n)[0:NS, 0:NS]), n)
                    if b < DEC_B:
                        act.wait_ge(smax_s, b + 1)
                        act.activation(sS[0:NS, b % 2, PAST:], self_scores[0:NS, b, :], ACT.Exp, scale=MLA_SCALE,
                                       bias=rmax[0:NS, 2 + b % 2:3 + b % 2], accum_out=sum5[0:NS, b % 2, 4:5])
                        for g in range(4):
                            n = batch_job(b, g)
                            give(act.activation(sS[0:NS, b % 2, 512 * g:512 * g + 512], bank(n)[0:NS, :], ACT.Exp,
                                                scale=MLA_SCALE, bias=rmax[0:NS, 2 + b % 2:3 + b % 2],
                                                accum_out=sum5[0:NS, b % 2, g:g + 1]), n)
                    if b > 0:
                        n = job(f"Ob{b - 1}")
                        take(act, n)
                        give(act.copy(oTs[:, :, b - 1, :], bank(n, NH, DEC_T)), n)

            if LAYERS > 1:
                odd()
                norm(2)
                mixture(1)

        @block.vector
        def _(dve):
            step = stepper(dve, dve_step)

            def row_stats(tile):
                r = ROWS[tile]
                for half in range(2):
                    i = dve.bn_stats(bn6[0:r, tile, half, :], acc[0:r, tile, 512 * half:512 * half + 512])
                return i

            def norm(k):
                dve.wait_ge(ln_stats, k + 1)
                for tile in range(NT):
                    r = ROWS[tile]
                    i = dve.bn_aggr(mv[0:r, tile, :], bn6[0:r, tile, :, :])
                step(i)
                dve.tensor_scalar(rstd, mv[:, :, 1], LN_EPS, None, ALU.add).then_inc(ln_var, 1)
                dve.wait_ge(ln_std, k + 1)
                step(dve.reciprocal(rstd, rstd))
                dve.scalar_tensor_tensor(nmr, mv[:, :, 0], -1.0, rstd, ALU.mult, ALU.mult).then_inc(ln_affine, 1)
                dve.wait_ge(ln_loaded, 16 * (k + 1))
                for tile in range(NT):
                    r = ROWS[tile]
                    dve.wait_ge(ln_scaled, NT * k + tile + 1)
                    step(dve.tensor_tensor(x[0:r, tile, :], x[0:r, tile, :], lnp[0:r, 0:D_MODEL], ALU.mult))
                    dve.tensor_tensor(x[0:r, tile, :], x[0:r, tile, :], lnp[0:r, D_MODEL:], ALU.add).then_inc(ln_done, 1)

            def residual(name):
                for half in range(2):
                    for tile in range(NT):
                        r = ROWS[tile]
                        n = job(name, NT * half + tile)
                        take(dve, n)
                        cols = slice(512 * half, 512 * half + 512)
                        give(dve.scalar_tensor_tensor(acc[0:r, tile, cols], x[0:r, tile, cols], ALPHA, bank(n)[0:r, :],
                                                      ALU.mult, ALU.add), n)
                        if half == 1 and tile > 0:
                            landed(dve, n - 1, 1)
                            row_stats(tile - 1)
                landed_all(dve, name)
                row_stats(NT - 1).then_inc(ln_stats, 1)

            def first_of(out, key, width):
                step(dve.tensor_reduce(s1, key, AX.X, ALU.max))
                step(dve.tensor_tensor(out, key, s1.unsqueeze(2).broadcast_to([P, NT, width]), ALU.is_equal))
                iota = c("iota")[:, 0:width].unsqueeze(1).broadcast_to([P, NT, width])
                step(dve.tensor_tensor(out, out, iota, ALU.mult))
                step(dve.tensor_reduce(s1, out, AX.X, ALU.min))
                step(dve.tensor_tensor(out, iota, s1.unsqueeze(2).broadcast_to([P, NT, width]), ALU.is_equal))

            def route(layer):
                n = job(f"{layer}.router")
                landed(dve, n, 1)
                dve.wait_ge(router_loaded, 32)
                step(dve.tensor_tensor(biased, score, rbias.unsqueeze(1).broadcast_to([P, NT, N_EXP]), ALU.add))
                b4 = biased.rearrange("p t (g e) -> p t g e", g=NG)
                first = True
                for i in range(EPG):
                    for j in range(i + 1, EPG):
                        step(dve.tensor_tensor(gs if first else gt, b4[:, :, :, i], b4[:, :, :, j], ALU.add))
                        if not first:
                            step(dve.tensor_tensor(gs, gs, gt, ALU.max))
                        first = False
                first_of(gm, gs, NG)
                gmb = gm.unsqueeze(3).broadcast_to([P, NT, NG, EPG])
                v4 = lambda a: a.rearrange("p t (g e) -> p t g e", g=NG)
                step(dve.tensor_scalar(gt, gm, BIG, -BIG, ALU.mult, ALU.add))
                step(dve.tensor_tensor(v4(t0), v4(biased), gmb, ALU.mult))
                step(dve.tensor_tensor(v4(t0), v4(t0), gt.unsqueeze(3).broadcast_to([P, NT, NG, EPG]), ALU.add))
                first_of(sel, t0, N_EXP)
                step(dve.scalar_tensor_tensor(t0, sel, -2 * BIG, t0, ALU.mult, ALU.add))
                first_of(t1, t0, N_EXP)
                dve.tensor_tensor(both, sel, t1, ALU.add).then_inc(sel_ready, 1)
                dve.wait_ge(sel_ready, layer + 1)
                step(dve.tensor_tensor(gates, both, score, ALU.mult))
                step(dve.tensor_reduce(s2, gates, AX.X, ALU.add))
                step(dve.reciprocal(s2, s2))
                dve.tensor_tensor(gates, gates, s2.unsqueeze(2).broadcast_to([P, NT, N_EXP]), ALU.mult)\
                    .then_inc(gates_ready, 1)
                dve.wait_ge(gates_ready, layer + 1)
                n = job(f"{layer}.pos")
                take(dve, n)
                pos = bank(n, NT + 1, N_EXP)
                base = c("rowbase")
                dve.tensor_tensor(t0[:, 0:4], pos[:, 0:4], base.unsqueeze(1).broadcast_to([P, 4, N_EXP]), ALU.add)
                dve.tensor_tensor(t0[0:NS, 4], pos[0:NS, 4], base[0:NS], ALU.add)
                give(dve.tensor_copy(total, pos[:, NT]), n)
                landed(dve, n, 1)
                for k, one in enumerate((sel, t1)):
                    step(dve.tensor_tensor(biased, one, t0, ALU.mult))
                    step(dve.tensor_reduce(row[:, :, k], biased, AX.X, ALU.add))
                    step(dve.tensor_tensor(biased, one, gates, ALU.mult))
                    step(dve.tensor_reduce(gate2[:, :, k], biased, AX.X, ALU.add))
                step(dve.tensor_copy(rowi[:, :], row.rearrange("p t k -> p (t k)")))
                step(dve.tensor_reduce(s1[:, 0:1], total, AX.X, ALU.max))
                step(dve.tensor_scalar(s1[:, 0:1], s1[:, 0:1], float(P), None, ALU.is_gt))
                dve.tensor_copy(crowded[0:1, 0:1], s1[0:1, 0:1]).then_inc(rows_ready, 1)

            def mixture(layer):
                L = f"{layer}."
                route(layer)
                for tile in range(NT):
                    r = ROWS[tile]
                    i = dve.tensor_scalar(acc[0:r, tile, :], x[0:r, tile, :], ALPHA, None, ALU.mult)
                step(i)
                flag = is_crowded(dve, layer)
                with dve.If(flag > 0):
                    for e in range(N_EXP):
                        for m in range(2):
                            for s, (a, nn) in enumerate(SPLITS):
                                n = job(f"{L}e{e}", 4 * m + 2 * s)
                                landed(dve, n, 1)
                                take(dve, n + 1)
                                give(dve.tensor_tensor(hT[:, e % 2, m, a:a + nn], hg[:, e % 2, m, a:a + nn],
                                                       bank(n + 1)[:, 0:nn], ALU.mult), n + 1)
                        for half in range(2):
                            for tile in range(NT):
                                r = ROWS[tile]
                                n = job(f"{L}e{e}", 8 + NT * half + tile)
                                take(dve, n)
                                cols = slice(512 * half, 512 * half + 512)
                                give(dve.scalar_tensor_tensor(acc[0:r, tile, cols], bank(n)[0:r, :], gates[0:r, tile, e:e + 1],
                                                              acc[0:r, tile, cols], ALU.mult, ALU.add), n)
                    landed_all(dve, f"{L}e{N_EXP - 1}")
                    for tile in range(NT):
                        i = row_stats(tile)
                    i.then_inc(ln_stats, 1)
                with dve.Else():
                    for e in range(-1, N_EXP + 1):
                        if e + 1 < N_EXP:
                            n = ejob(layer, e + 1, "T1")
                            take(dve, n)
                            give(dve.tensor_copy(xgT[:, (e + 1) % 2, 4:8, :], bank(n, 4, P)), n)
                        if 0 <= e < N_EXP:
                            n = ejob(layer, e, "GU")
                            dve.wait_ge(silu_done[layer], e + 1)
                            give(dve.tensor_tensor(hS[:, e % 2, :], hgS, bank(n)[:, D_EXP:], ALU.mult), n)
                        if e > 0:
                            n = ejob(layer, e - 1, "D1")
                            if e - 1 >= NYS:
                                dve.wait_ge(y_stored[layer][(e - 1) % NYS], 16 * ((e - 1) // NYS))
                            take(dve, n)
                            give(dve.tensor_copy(yS[:, (e - 1) % NYS, 512:], bank(n)), n)
                    def combine(tile, k):
                        r = ROWS[tile]
                        dve.scalar_tensor_tensor(acc[0:r, tile, :], yg[0:r, tile, k, :], gate2[0:r, tile, k:k + 1],
                                                 acc[0:r, tile, :], ALU.mult, ALU.add).then_inc(combined[layer], 1)

                    for tile in range(NT):
                        dve.wait_ge(gathered[layer][tile], 32)
                        combine(tile, 0)
                        if tile > 0:
                            dve.wait_ge(combined[layer], 2 * tile)
                            row_stats(tile - 1)
                        dve.wait_ge(combined[layer], 2 * tile + 1)
                        combine(tile, 1)
                    dve.wait_ge(combined[layer], 2 * NT)
                    row_stats(NT - 1).then_inc(ln_stats, 1)
                    landed(dve, ejob(layer, N_EXP - 1, "D1") - NBANK + 1, NBANK)
                    skipped = (N_EXP * (8 + 2 * NT) - N_EXP * len(SPARSE)) // NBANK
                    for b in range(NBANK):
                        dve.sem_inc(filled[b], skipped)
                        dve.sem_inc(emptied[b], skipped)
                    for s in range(NSLOT):
                        first = FIRST_EXPERT_BLOCK[layer]
                        dve.sem_inc(slot_loaded[s], 16 * sum(1 for j in range(NSLOT, 3 * N_EXP) if (first + j) % NSLOT == s))
                norm(2 * layer + 1)

            dve.memset(aP[:, :, 0:16], 0.0)
            dve.memset(stat[:, :], 0.0)
            dve.memset(vmv, 0.0)
            dve.memset(zero, 0.0)
            step(dve.memset(acc_t[:, :], 0.0))
            dve.memset(aS[:, :, :, 0:1], 0.0).then_inc(cleared, 1)
            dve.wait_ge(const_loaded, 16)
            dve.wait_ge(even_loaded, 16)
            step(dve.tensor_tensor(WT, WT, c("triu").unsqueeze(1).broadcast_to([P, HB, P]), ALU.mult))
            dve.tensor_tensor(WTs[0:NS], WTs[0:NS], c("triu", NS)[:, 0:NS].unsqueeze(1).broadcast_to([NS, HB, NS]),
                              ALU.mult).then_inc(mask_applied, 1)
            dve.wait_ge(buf_loaded, 16)
            dve.wait_ge(cleared, 1)
            dve.tensor_copy(aS[:, :, :, 0:POOL_BUF], bufT).then_inc(buf_in_place, 1)
            dve.wait_ge(buf_in_place, 1)
            for m in range(4):
                for s in range(2):
                    n = job("au", 2 * m + s)
                    take(dve, n)
                    if s == 0:
                        give(dve.tensor_copy(aP[:, m, 16:], bank(n)), n)
                    else:
                        give(dve.tensor_copy(aS[:, m, :, POOL_BUF:], bank(n, DEC_B, DEC_T)), n)
            landed(dve, job("au"), 8)
            for g, w in enumerate(WINDOWS):
                for s, (src, tmp, shape, skip) in enumerate(((aP, sumP, None, 16), (aS, sumS, DEC_B, POOL_BUF))):
                    cur = src[:, g]
                    own = cur
                    width = cur.shape[-1]
                    for lev in range(g + 1):
                        sh = 1 << lev
                        lo = 2 * sh - 1
                        new = tmp[:, lev % 2]
                        if s == 0:
                            step(dve.tensor_tensor(new[:, lo:], cur[:, lo:], cur[:, lo - sh:width - sh], ALU.add))
                        else:
                            step(dve.tensor_tensor(new[:, :, lo:], cur[:, :, lo:], cur[:, :, lo - sh:width - sh], ALU.add))
                        cur = new
                    if s == 0:
                        step(dve.tensor_tensor(cur[:, 16:32], cur[:, 16:32],
                                               c("corr")[:, 16 * g:16 * g + 16], ALU.mult))
                        dve.scalar_tensor_tensor(pooled[:, g, 0:SEQ], cur[:, 16:], 1.0 / w, own[:, 16:],
                                                 ALU.mult, ALU.subtract).then_inc(pooled_ready, 1)
                    else:
                        dve.scalar_tensor_tensor(pooled[:, g, SEQ:T].rearrange("p (b t) -> p b t", b=DEC_B),
                                                 cur[:, :, POOL_BUF:], 1.0 / w, own[:, :, POOL_BUF:],
                                                 ALU.mult, ALU.subtract).then_inc(pooled_ready, 1)
            for tile in range(NT):
                r = ROWS[tile]
                landed(dve, job("v", tile), 1)
                for h in range(HB):
                    i = dve.bn_stats(vstat[0:r, tile, h, :], vn[0:r, tile, P * h:P * h + P])
            step(i)
            for tile in range(NT):
                r = ROWS[tile]
                for h in range(HB):
                    i = dve.bn_aggr(vmv[0:r, tile, h, :], vstat[0:r, tile, h, :])
            step(i)
            dve.tensor_scalar(vrstd, vmv[:, :, :, 1], LN_EPS, None, ALU.add).then_inc(vn_var, 1)
            dve.wait_ge(vn_std, 1)
            step(dve.reciprocal(vrstd, vrstd))
            for tile in range(NT):
                r = ROWS[tile]
                for h in range(HB):
                    i = dve.tensor_scalar(vn[0:r, tile, P * h:P * h + P], vn[0:r, tile, P * h:P * h + P],
                                          vmv[0:r, tile, h, 0:1], vrstd[0:r, tile, h:h + 1], ALU.subtract, ALU.mult)
                step(i)
                step(dve.tensor_tensor(vn[0:r, tile, :], vn[0:r, tile, :], sgg[0:r, :], ALU.mult))
                dve.tensor_tensor(vn[0:r, tile, :], vn[0:r, tile, :], sgb[0:r, :], ALU.add).then_inc(vn_ready, 1)
            landed(dve, job("au"), 16)
            for tile in range(NT):
                r = ROWS[tile]
                n = job("mix", tile)
                take(dve, n)
                dst = cat[:, HB:, tok(tile)]
                bias = sbias if tile < NT - 1 else sbiasS
                step(dve.tensor_tensor(dst, bank(n, HB, P)[:, :, 0:r], bias, ALU.add))
                give(dve.tensor_tensor(dst, dst, uT[:, :, tok(tile)], ALU.mult), n)
            dve.wait_ge(x_loaded, 16)
            residual("0.out")
            norm(0)
            mixture(0)

            def mulb(out, a, b, op=ALU.mult):
                return dve.tensor_tensor(out, a, b, op)

            def odd():
                dve.wait_ge(table_loaded, 32)
                kf = rtmp[:, 0].rearrange("p n e -> p (n e)")[:, 0:4 * DEC_B]
                step(dve.tensor_copy(kf, kpe_row[:, :]))
                step(dve.tensor_scalar(kf, kf, float(D_ROPE), c("lane")[:, 0:1], ALU.mult, ALU.add))
                dve.tensor_copy(kpe_row[:, :], kf).then_inc(kpe_rows, 1)
                dve.wait_ge(rwkv_loaded, 16)
                tail = lambda m: pc[:, m % 2, 1 + SEQ:].rearrange("p (b t) -> p b t", b=DEC_B)

                def begin(m):
                    dve.memset(pc[:, m % 2, 0:1], 0.0)
                    dve.tensor_copy(tail(m)[:, :, 0], shift[:, m, :]).then_inc(pc_begun, 1)

                begin(0)
                begin(1)
                for m in range(CT):
                    landed(dve, job("c", 2 * m), 2)
                    dve.wait_ge(pc_begun, m + 1)
                    p_, t_ = pc[:, m % 2, :], tail(m)
                    xsS = xs[:, m, SEQ:].rearrange("p (b t) -> p b t", b=DEC_B)
                    dve.tensor_tensor(xs[:, m, 0:SEQ], p_[:, 0:SEQ], p_[:, 1:1 + SEQ], ALU.subtract)
                    dve.tensor_copy(shout[:, m, 0:1], p_[:, SEQ:SEQ + 1])
                    dve.tensor_copy(shout[:, m, 1:9], t_[:, :, DEC_T])
                    step(dve.tensor_tensor(xsS, t_[:, :, 0:DEC_T], t_[:, :, 1:], ALU.subtract))
                    dve.scalar_tensor_tensor(xs[:, m, 0:SEQ], xs[:, m, 0:SEQ], mu[:, m:m + 1], p_[:, 1:1 + SEQ],
                                             ALU.mult, ALU.add)
                    dve.scalar_tensor_tensor(xsS, xsS, mu[:, m:m + 1], t_[:, :, 1:], ALU.mult, ALU.add)\
                        .then_inc(xs_ready, 1)
                    if m + 2 < CT:
                        dve.wait_ge(xs_ready, m + 1)
                        begin(m + 2)
                for tile in range(NT):
                    r = ROWS[tile]
                    n = job("dtok", tile)
                    take(dve, n)
                    give(dve.tensor_copy(pd[0:r, tile, :], bank(n)[0:r, 0:D_COLS]), n)
                landed_all(dve, "dtok")
                for tile in range(NT):
                    r = ROWS[tile]
                    for k, (a, b) in enumerate(((0, Q_LORA), (Q_LORA, Q_LORA + KV_LORA))):
                        i = dve.tensor_tensor_reduce(junk[0:r, k, 0:b - a], pd[0:r, tile, a:b], pd[0:r, tile, a:b], 1.0, 0.0,
                                                     ALU.mult, ALU.add, ss[0:r, tile, k:k + 1])
                        step(i)
                dve.tensor_scalar(srs[:, :, 0], ss[:, :, 0], 1.0 / Q_LORA, RMS_EPS, ALU.mult, ALU.add)
                dve.tensor_scalar(srs[:, :, 1], ss[:, :, 1], 1.0 / KV_LORA, RMS_EPS, ALU.mult, ALU.add)\
                    .then_inc(rms_sum, 1)
                half = D_ROPE // 2
                cos, sin = (c(k).rearrange("p (n e) -> p n e", n=NT) for k in ("cos", "sin"))
                k1, k2 = pd[:, :, Q_LORA + KV_LORA:Q_LORA + KV_LORA + half], pd[:, :, Q_LORA + KV_LORA + half:]
                for dst, (u, v, op) in ((slice(0, half), (cos, sin, ALU.subtract)), (slice(half, 2 * half), (sin, cos, ALU.add))):
                    dve.tensor_tensor(rtmp[:, 0], k1, u, ALU.mult)
                    step(dve.tensor_tensor(rtmp[:, 1], k2, v, ALU.mult))
                    step(dve.tensor_tensor(kp4[:, :, 0, dst], rtmp[:, 0], rtmp[:, 1], op))
                for k in range(1, 4):
                    i = dve.tensor_copy(kp4[:, :, k, :], kp4[:, :, 0, :])
                step(i)
                step(dve.tensor_scalar(okac, kac, -1.0, 1.0, ALU.mult, ALU.add))
                for m in range(4):
                    i = dve.tensor_scalar(alpha[:, m, :], K_[:, m, :], kkc[:, m:m + 1], None, ALU.mult)
                step(i)
                dve.tensor_tensor(rho, alpha, alpha, ALU.mult).then_inc(sq_ready, 1)
                dve.wait_ge(rms_std, 1)
                step(dve.reciprocal(srs, srs))
                dve.memset(ckv[NS:P, NT - 1, :], 0.0)
                for tile in range(NT):
                    r = ROWS[tile]
                    dve.scalar_tensor_tensor(ckv[0:r, tile, :], pd[0:r, tile, Q_LORA:Q_LORA + KV_LORA],
                                             srs[0:r, tile, 1:2], gkv[0:r, :], ALU.mult, ALU.mult)
                    i = dve.scalar_tensor_tensor(pd[0:r, tile, 0:Q_LORA], pd[0:r, tile, 0:Q_LORA], srs[0:r, tile, 0:1],
                                                 gq[0:r, :], ALU.mult, ALU.mult)
                i.then_inc(mla_rows, 1)

                for tile in range(NT):
                    r = ROWS[tile]
                    n = job("decay", tile)
                    take(dve, n)
                    give(dve.tensor_tensor(ld[0:r, tile, :], bank(n)[0:r, :], w0[0:r, :], ALU.add), n)
                for m in range(4):
                    for s, (a, nn) in enumerate(SPLITS):
                        n = job("norm", 2 * m + s)
                        take(dve, n)
                        give(dve.tensor_scalar(rho[:, m, a:a + nn], bank(n)[:, 0:nn], 1e-12, None, ALU.add), n)
                landed_all(dve, "norm")
                dve.reciprocal(rho, rho).then_inc(kk_sum, 1)
                landed_all(dve, "iclr")
                landed_all(dve, "dT")
                for m in range(4):
                    i = dve.tensor_scalar(kappa[:, m, :], beta[:, m, :], kac[:, m:m + 1], okac[:, m:m + 1],
                                          ALU.mult, ALU.add)
                step(i)
                step(mulb(kappa, kappa, K_))
                mulb(K_, R_, kappa).then_inc(bonus_in, 1)
                dve.wait_ge(kk_std, 1)
                step(mulb(alpha, alpha, rho))
                step(mulb(beta, beta, alpha))
                n = job("bonus")
                take(dve, n)
                dve.tensor_copy(bon[:, 0:4, :], bank(n, NT, NH)[:, 0:4, :])
                give(dve.tensor_copy(bon[0:NS, 4, :], bank(n, NT, NH)[0:NS, 4, :]), n)
                for tile in range(NT):
                    r = ROWS[tile]
                    for q in range(2):
                        i = 2 * tile + q
                        landed(dve, job("cum", i), 1)
                        e = expo[:, i % 2, :, :, 0:r]
                        at = (slice(None), slice(2 * q, 2 * q + 2), tok(tile))
                        mulb(alpha[at], alpha[at], e[:, 1])
                        mulb(rho[at], R_[at], e[:, 0])
                        mulb(beta[at], beta[at], e[:, 2])
                        mulb(kappa[at], kappa[at], e[:, 2])
                        if r == P:
                            i = dve.tensor_copy(dec[:, 2 * q:2 * q + 2, 2 * tile:2 * tile + 2], e[:, 0, :, CH - 1::CH])
                        else:
                            i = dve.tensor_copy(decS[:, 2 * q:2 * q + 2, :], e[:, 0, :, DEC_T - 1::DEC_T])
                        i.then_inc(scaled_ready, 1)
                dve.wait_ge(scaled_ready, 2 * NT)
                dve.memset(stateP, 0.0).then_inc(state_reset, 1)
                dve.wait_ge(state_reset, 1)
                dve.wait_ge(stored, 16 * 6)
                dve.wait_ge(state_loaded, 16)
                for tile in range(NT):
                    recurrence(tile)
                latent_attention()

            def recurrence(tile):
                r = ROWS[tile]
                prompt = tile < NT - 1
                mask = {"Nd": "mNd", "No": "mNo", "M": "mMd", "G2": "mG2", "G3": "mG3", "G4": "mG4"} if prompt else \
                       {"Nd": "sNd", "M": "sMd", "G2": "sNd", "G3": "sG3", "G4": "sG4"}
                four = lambda name: c(mask[name], r).unsqueeze(1).broadcast_to([r, 4, r])
                for k in (1, 3):
                    n = job(f"tok{tile}", k)
                    take(dve, n)
                    give(dve.tensor_copy(tokm[0:r, k].rearrange("p a s v -> p a (s v)"), bank(n, 4, P)[0:r, :, :]), n)
                for step_name in (STEPS if prompt else STEPS_S):
                    for s in range(2):
                        n = unit_job(tile, step_name, s)
                        d = {k: v[0:r, :, 0:r] for k, v in sm[s].items() if k not in ("U", "GV", "UG")}
                        src = bank(n, 4, P)[0:r, :, 0:r]
                        if step_name == "MT":
                            take(dve, n)
                            if prompt:
                                dve.tensor_tensor(d["No"], src, four("No"), ALU.mult)
                            give(dve.tensor_tensor(d["Nd"], src, four("Nd"), ALU.mult), n)
                            landed(dve, n, 1)
                            dve.tensor_tensor(d["XA"], c("ident", r)[:, 0:r].unsqueeze(1).broadcast_to([r, 4, r]), d["Nd"],
                                              ALU.subtract).then_inc(x0_ready, 1)
                        elif step_name in ("M", "G2", "G3", "G4"):
                            take(dve, n)
                            dst = d["Md" if step_name == "M" else step_name]
                            give(dve.tensor_tensor(dst, src, four(step_name), ALU.mult), n)
                        elif step_name in ("X1", "X2", "X3", "Z", "TT"):
                            take(dve, n)
                            if step_name == "X1":
                                dve.wait_ge(x0_ready, 2 * tile + s + 1)
                            else:
                                before = {"X2": "X1", "X3": "X2", "Z": "X3", "TT": "Z"}[step_name]
                                landed(dve, unit_job(tile, before, s), 1)
                            a, b = {"X1": ("XB", "XA"), "X2": ("XA", "XB"), "X3": ("XB", "XA"), "Z": ("XA", "XB"),
                                    "TT": ("TT", "XA")}[step_name]
                            give(dve.tensor_tensor(d[a], d[b], src, ALU.subtract if step_name == "TT" else ALU.add), n)
                ybn = bank
                if prompt:
                    for ch in range(2):
                        rc = slice(CH * ch, CH * ch + CH)
                        for s in range(2):
                            n = job(f"chain{tile}", 3 * ch + s)
                            landed(dve, unit_job(tile, "U", s), 1)
                            take(dve, n)
                            dve.tensor_tensor(p_sb[rc, :, s, :], bank(n, 2, 4, HD)[rc, 0], sm[s]["U"][rc], ALU.add)
                            give(dve.tensor_copy(y_sb[rc, :, s, :], bank(n, 2, 4, HD)[rc, 1]), n)
                        n = job(f"chain{tile}", 3 * ch + 2)
                        take(dve, n)
                        step(dve.tensor_tensor(stateP, stateP, bank(n, 4, HD), ALU.add))
                        w = dec[:, :, 2 * tile + ch:2 * tile + ch + 1].broadcast_to([P, 4, HD])
                        give(dve.tensor_tensor(stateP, stateP, w, ALU.mult), n)
                        landed(dve, n, 1)
                else:
                    own = c("ofbatch", r).unsqueeze(2).broadcast_to([r, DEC_B, HD])
                    def own_states(h):
                        j, s = h // 2, h % 2
                        d = {k: sm[s][k][0:r].rearrange("p a b -> p (a b)").rearrange("p (b v) -> p b v", b=DEC_B)
                             for k in ("N4", "M8", "No", "Md")}
                        for k, (tmp, dst) in enumerate((("N4", p_sb), ("M8", y_sb))):
                            n = state_job(h, k)
                            take(dve, n)
                            give(dve.tensor_tensor(d[tmp], bank(n, DEC_B, HD)[0:r], own, ALU.mult), n)
                            landed(dve, n, 1)
                            step(dve.tensor_reduce(dst[0:r, j, s, :], d[tmp].rearrange("p b v -> p v b"), AX.X, ALU.add))
                        if h < 2:
                            landed(dve, unit_job(tile, "U", s), 1)
                        step(dve.tensor_tensor(p_sb[0:r, j, s, :], p_sb[0:r, j, s, :], sm[s]["U"][0:r, j, :], ALU.add))
                        dve.tensor_tensor(d["No"], p_sb[0:r, j, s, :].unsqueeze(1).broadcast_to([r, DEC_B, HD]), own, ALU.mult)
                        dve.tensor_tensor(d["Md"], tokm[0:r, 1, j, s, :].unsqueeze(1).broadcast_to([r, DEC_B, HD]), own,
                                          ALU.mult).then_inc(psel_ready, 1)

                    own_states(0)
                    for h in range(NH):
                        j, s = h // 2, h % 2
                        p0 = slice(HD * s, HD * s + HD)
                        if h + 1 < NH:
                            own_states(h + 1)
                        n = state_job(h, 2)
                        take(dve, n)
                        step(dve.tensor_tensor(stateS[p0, j], stateS[p0, j], bank(n, DEC_B, HD)[p0], ALU.add))
                        w = decS[p0, j, :].unsqueeze(2).broadcast_to([HD, DEC_B, HD])
                        give(dve.tensor_tensor(stateS[p0, j], stateS[p0, j], w, ALU.mult), n)
                y = y_sb[0:r].rearrange("p a s v -> p (a s) v")
                p_ = p_sb[0:r].rearrange("p a s v -> p (a s) v")
                bc = lambda a: a.unsqueeze(2).broadcast_to([r, NH, HD])
                n = job(f"y{tile}", 0)
                take(dve, n)
                give(dve.tensor_tensor(y, y, bank(n, NH, HD)[0:r], ALU.add), n)
                landed(dve, n, 1)
                for h in range(NH):
                    i = dve.bn_stats(gn6[0:r, h, :], y[:, h, :])
                step(i)
                for h in range(NH):
                    i = dve.bn_aggr(gmv[0:r, h, :], gn6[0:r, h, :])
                step(i)
                dve.tensor_scalar(grs[0:r], gmv[0:r, :, 1], GN_EPS, None, ALU.add).then_inc(gn_var, 1)
                step(dve.tensor_tensor(p_, tokm[0:r, 1].rearrange("p a s v -> p (a s) v"), bc(bon[0:r, tile, :]), ALU.mult))
                step(dve.tensor_tensor(y, y, bc(gmv[0:r, :, 0]), ALU.subtract))
                dve.wait_ge(gn_std, tile + 1)
                step(dve.reciprocal(grs[0:r], grs[0:r]))
                step(dve.tensor_tensor(y, y, bc(grs[0:r]), ALU.mult))
                step(dve.tensor_tensor(y, y, gng[0:r].rearrange("p a s v -> p (a s) v"), ALU.mult))
                step(dve.tensor_tensor(y, y, gnb[0:r].rearrange("p a s v -> p (a s) v"), ALU.add))
                step(dve.tensor_tensor(y, y, p_, ALU.add))
                n = job(f"y{tile}", 1)
                take(dve, n)
                give(dve.tensor_tensor(y, y, bank(n, NH, HD)[0:r], ALU.mult), n)
                take(dve, job(f"yT{tile}"))

            def latent_attention():
                tmp = pP[:, 0, :]
                for g in range(2):
                    for s, (a, nn) in enumerate(SPLITS):
                        n = job("qpe", 4 * g + 2 * s)
                        take(dve, n)
                        give(dve.tensor_tensor(qpeT[:, g, a:a + nn], bank(n)[:, 0:nn], c("cosT")[:, a:a + nn], ALU.mult), n)
                        n += 1
                        take(dve, n)
                        give(dve.tensor_tensor(tmp[:, 0:nn], bank(n)[:, 0:nn], c("sinT")[:, a:a + nn], ALU.mult), n)
                        landed(dve, n - 1, 2)
                        step(dve.tensor_tensor(qpeT[:, g, a:a + nn], qpeT[:, g, a:a + nn], tmp[:, 0:nn], ALU.add))
                for g in range(4):
                    for i in range(4):
                        for hh in range(2):
                            src = qpeT[32 * i:32 * i + 32, hh, SEQ:T].rearrange("p (b t) -> p b t", b=DEC_B)
                            ins = dve.tensor_copy(qpeS[32 * g:32 * g + 32, :, 4 * hh + i, :], src)
                step(ins)
                dve.memset(rinv[:, 0:1], 0.0).then_inc(qpe_ready, 1)

                def peak(u):
                    t = u % 4
                    n = job(f"S{u}")
                    take(dve, n)
                    diag = bank(n)[:, P * t:P * t + P]
                    step(dve.tensor_tensor(diag, diag, c("negtri"), ALU.add))
                    step(dve.tensor_reduce(rmax[:, u % 2:u % 2 + 1], bank(n)[:, 0:P * t + P], AX.X, ALU.max))
                    dve.tensor_scalar(rmax[:, u % 2:u % 2 + 1], rmax[:, u % 2:u % 2 + 1], -MLA_SCALE, None, ALU.mult)\
                        .then_inc(smax, 1)

                def normalise(u):
                    landed(dve, job(f"S{u}"), 1)
                    keys = P * (u % 4 + 1)
                    step(dve.reciprocal(rinv[:, u % 2:u % 2 + 1], rsum[:, u % 2:u % 2 + 1]))
                    dve.tensor_scalar(pP[:, u % 3, 0:keys], pP[:, u % 3, 0:keys], rinv[:, u % 2:u % 2 + 1], None,
                                      ALU.mult).then_inc(snorm, 1)

                for u in range(N_ATT + LAG + 2):
                    if u < N_ATT:
                        peak(u)
                    if 1 <= u <= N_ATT:
                        normalise(u - 1)
                    if u - LAG - 2 >= 0 and (u - LAG - 2) % 4 == 3:
                        h = (u - LAG - 2) // 4
                        p0 = slice(HD * (h % 2), HD * (h % 2) + HD)
                        n = job(f"yd{h}")
                        take(dve, n)
                        give(dve.tensor_copy(cat[p0, 4 + h // 2, 0:SEQ], bank(n)[p0, :]), n)

                step(dve.memset(qpeG, 0.0))
                for g in range(4):
                    q = slice(32 * g, 32 * g + 32)
                    i = dve.tensor_copy(qpeG[q, g], qpeS[q].rearrange("p b h t -> p b (h t)"))
                i.then_inc(groups_ready, 1)
                n = job("own")
                take(dve, n)
                give(dve.tensor_tensor(self_scores[0:NS], bank(n, DEC_B, NS)[0:NS], c("negS", NS).rearrange("p (b k) -> p b k", b=DEC_B),
                                       ALU.add), n)
                landed(dve, n, 1)
                dve.tensor_reduce(max5[0:NS, :, 4], self_scores[0:NS], AX.X, ALU.max)

                for b in range(DEC_B + 1):
                    if b > 0:
                        v = b - 1
                        landed(dve, batch_job(v, 3), 1)
                        if v >= 1:
                            landed_all(dve, f"PTb{v - 1}")
                        step(dve.tensor_reduce(rinv[0:NS, 2:3], sum5[0:NS, v % 2, :], AX.X, ALU.add))
                        step(dve.reciprocal(rinv[0:NS, 2:3], rinv[0:NS, 2:3]))
                        dve.tensor_scalar(diag_s[0:NS, :], ident[0:NS, 0:NS], rinv[0:NS, 2:3], None, ALU.mult)\
                            .then_inc(snorm_s, 1)
                    if b < DEC_B:
                        for g in range(4):
                            n = batch_job(b, g)
                            take(dve, n)
                            i = dve.tensor_reduce(max5[0:NS, b, g:g + 1], bank(n)[0:NS, :], AX.X, ALU.max)
                        step(i)
                        m = rmax[0:NS, 2 + b % 2:3 + b % 2]
                        step(dve.tensor_reduce(m, max5[0:NS, b, :], AX.X, ALU.max))
                        dve.tensor_scalar(m, m, -MLA_SCALE, None, ALU.mult).then_inc(smax_s, 1)
                n = job("ydS")
                take(dve, n)
                give(dve.tensor_copy(cat[:, 4:8, SEQ:T], bank(n, 4, NS)), n)

            if LAYERS > 1:
                odd()
                residual("1.out")
                norm(2)
                mixture(1)




def kernel(**inputs):
    import concourse.bacc as _bacc
    from concourse.bass_utils import run_bass_kernel_spmd as _run

    nc = _bacc.Bacc("TRN2", target_bir_lowering=False, num_devices=1)
    arrays, args, outs = {}, {}, {}
    for name, a in lay_out(inputs).items():
        a = np.ascontiguousarray(a)
        arrays[f"in_{name}_dram"] = a
        args[name] = nc.dram_tensor(f"in_{name}_dram", a.shape, mybir.dt.from_np(a.dtype), kind="ExternalInput").ap()
    for name, shape in OUTS.items():
        outs[name] = nc.dram_tensor(f"out_{name}_dram", shape, F32, kind="ExternalOutput").ap()
    program(nc, args, outs)
    r = _run(nc, [arrays], core_ids=[0])
    return lay_back({name: np.asarray(r.results[0][f"out_{name}_dram"]) for name in OUTS})
```
